# Optimizing a Trainium2 kernel written in Bass

```python
import jax, jax.numpy as jnp
from jax import lax
import numpy as np

D_MODEL = 1024
BATCH = 1
SEQ = 512
DEPTH = 2

N_MIXERS = 2
HEAD_DIM = 64
N_HEADS = D_MODEL // HEAD_DIM
DILATED_GROUPS = ((128, 1), (512, 4), (2048, 16))
N_GROUPS = len(DILATED_GROUPS)
ROPE_THETA = 500000.0
ROPE_DIM = HEAD_DIM // 4
BLK = 64
CONV_WIDTH = 3
FFN_HIDDEN = -(-8 * D_MODEL // (3 * 256)) * 256
NORM_EPS = 1e-6
NEG_INF = -1e30

kernel_name = "hybrid_dilated_attn_shortconv_adaln_encoder"

def rms_norm(x, g):
    xf = x.astype(jnp.float32)
    r = lax.rsqrt(jnp.mean(xf * xf, axis=-1, keepdims=True) + NORM_EPS)
    return (xf * r).astype(x.dtype) * g

def modulate(h, shift, scale):
    return h * (1 + scale) + shift

def rope_partial(x, pos):
    half = ROPE_DIM // 2
    inv = ROPE_THETA ** (-jnp.arange(half, dtype=jnp.float32) * (2.0 / ROPE_DIM))
    ang = pos.astype(jnp.float32)[:, None] * inv[None, :]
    cos = jnp.cos(ang)[None, :, None, :]
    sin = jnp.sin(ang)[None, :, None, :]
    xr = x[..., :ROPE_DIM].astype(jnp.float32)
    x1, x2 = xr[..., :half], xr[..., half:]
    rot = jnp.concatenate([x1 * cos - x2 * sin, x2 * cos + x1 * sin], axis=-1).astype(x.dtype)
    return jnp.concatenate([rot, x[..., ROPE_DIM:]], axis=-1)

def banded_window_attention(q, k, v, half_window):
    N, L, H, Dh = q.shape
    nb = -(-L // BLK)
    Lp = nb * BLK
    qb = jnp.pad(q, ((0, 0), (0, Lp - L), (0, 0), (0, 0))).reshape(N, nb, BLK, H, Dh)

    def neighbourhood(t):
        t = jnp.pad(t, ((0, 0), (BLK, Lp - L + BLK), (0, 0), (0, 0))).reshape(N, nb + 2, BLK, H, Dh)
        return jnp.concatenate([t[:, :-2], t[:, 1:-1], t[:, 2:]], axis=2)

    kb, vb = neighbourhood(k), neighbourhood(v)
    qpos = jnp.arange(nb)[:, None] * BLK + jnp.arange(BLK)[None, :]
    kpos = jnp.arange(nb)[:, None] * BLK - BLK + jnp.arange(3 * BLK)[None, :]
    kp = kpos[:, None, :]
    mask = (jnp.abs(qpos[:, :, None] - kp) <= half_window) & (kp >= 0) & (kp < L)
    s = jnp.einsum('nbqhd,nbkhd->nbhqk', qb, kb, preferred_element_type=jnp.float32) * (Dh ** -0.5)
    s = jnp.where(mask[None, :, None], s, NEG_INF)
    m = jnp.max(s, axis=-1, keepdims=True)
    p = jnp.exp(s - m)
    l = jnp.sum(p, axis=-1, keepdims=True)
    o = jnp.einsum('nbhqk,nbkhd->nbqhd', p.astype(v.dtype), vb, preferred_element_type=jnp.float32)
    o = o / jnp.transpose(l, (0, 1, 3, 2, 4))
    lse = jnp.transpose((m + jnp.log(l))[..., 0], (0, 1, 3, 2))
    o = o.reshape(N, Lp, H, Dh)[:, :L]
    lse = lse.reshape(N, Lp, H)[:, :L]
    return o, lse

def dilated_attention(q, k, v, dilation, half_window):
    B, S, H, Dh = q.shape
    L = S // dilation

    def split(t):
        return t.reshape(B, L, dilation, H, Dh).transpose(0, 2, 1, 3, 4).reshape(B * dilation, L, H, Dh)

    o, lse = banded_window_attention(split(q), split(k), split(v), half_window)
    o = o.reshape(B, dilation, L, H, Dh).transpose(0, 2, 1, 3, 4).reshape(B, S, H, Dh)
    lse = lse.reshape(B, dilation, L, H).transpose(0, 2, 1, 3).reshape(B, S, H)
    return o, lse

def dilated_mixture_mixer(h, w_qkv, w_o, pos):
    B, S, _ = h.shape
    qkv = (h @ w_qkv).reshape(B, S, N_GROUPS, 3, N_HEADS, HEAD_DIM)
    outs, lses = [], []
    for g, (window, dil) in enumerate(DILATED_GROUPS):
        q = rope_partial(qkv[:, :, g, 0], pos)
        k = rope_partial(qkv[:, :, g, 1], pos)
        o, lse = dilated_attention(q, k, qkv[:, :, g, 2], dil, window // (2 * dil))
        outs.append(o)
        lses.append(lse)
    wts = jax.nn.softmax(jnp.stack(lses, axis=0), axis=0)
    o = jnp.einsum('gbsh,gbshd->bshd', wts, jnp.stack(outs, axis=0))
    return o.reshape(B, S, D_MODEL).astype(h.dtype) @ w_o

def short_conv_mixer(h, w_in, conv_w, w_out):
    b_gate, c_gate, u = jnp.split(h @ w_in, 3, axis=-1)
    z = lax.conv_general_dilated(
        c_gate * u, conv_w[:, None, :], window_strides=(1,),
        padding=[((CONV_WIDTH - 1) // 2, (CONV_WIDTH - 1) // 2)],
        dimension_numbers=('NWC', 'WIO', 'NWC'), feature_group_count=D_MODEL)
    return (b_gate * z) @ w_out

def swiglu_ffn(h, w_in, w_out):
    g, u = jnp.split(h @ w_in, 2, axis=-1)
    return (jax.nn.silu(g) * u) @ w_out

def setup_inputs(seed: int = 0) -> dict:
    key = jax.random.key(seed)
    ks = jax.random.split(key, 16)
    D, F = D_MODEL, FFN_HIDDEN
    n_a = (DEPTH + N_MIXERS - 1) // N_MIXERS
    n_b = DEPTH // N_MIXERS
    nrm = lambda k, shape, fan: jax.random.normal(k, shape, jnp.float32) * (fan ** -0.5)
    return {
        "x": jax.random.normal(ks[0], (BATCH, SEQ, D), jnp.float32),
        "c": jax.random.normal(ks[1], (BATCH, D), jnp.float32),
        "attn_w_qkv": nrm(ks[2], (n_a, D, N_GROUPS * 3 * D), D),
        "attn_w_o": nrm(ks[3], (n_a, D, D), D),
        "conv_w_in": nrm(ks[4], (n_b, D, 3 * D), D),
        "conv_w": nrm(ks[5], (n_b, CONV_WIDTH, D), CONV_WIDTH),
        "conv_w_out": nrm(ks[6], (n_b, D, D), D),
        "ada_w": nrm(ks[7], (DEPTH, D, 6 * D), D),
        "ada_b": 0.02 * jax.random.normal(ks[8], (DEPTH, 6 * D), jnp.float32),
        "norm_mix_g": 1.0 + 0.02 * jax.random.normal(ks[9], (DEPTH, D), jnp.float32),
        "norm_ffn_g": 1.0 + 0.02 * jax.random.normal(ks[10], (DEPTH, D), jnp.float32),
        "ffn_w_in": nrm(ks[11], (DEPTH, D, 2 * F), D),
        "ffn_w_out": nrm(ks[12], (DEPTH, F, D), F),
        "final_g": 1.0 + 0.02 * jax.random.normal(ks[13], (D,), jnp.float32),
    }

def reference(x, c, attn_w_qkv, attn_w_o, conv_w_in, conv_w, conv_w_out, ada_w, ada_b,
              norm_mix_g, norm_ffn_g, ffn_w_in, ffn_w_out, final_g):
    pos = jnp.arange(x.shape[1], dtype=jnp.int32)
    cond = jax.nn.silu(c)
    for i in range(DEPTH):
        mod = (cond @ ada_w[i] + ada_b[i])[:, None, :]
        sh1, sc1, g1, sh2, sc2, g2 = jnp.split(mod, 6, axis=-1)
        h = modulate(rms_norm(x, norm_mix_g[i]), sh1, sc1)
        j = i // N_MIXERS
        if i % N_MIXERS == 0:
            y = dilated_mixture_mixer(h, attn_w_qkv[j], attn_w_o[j], pos)
        else:
            y = short_conv_mixer(h, conv_w_in[j], conv_w[j], conv_w_out[j])
        x = x + g1 * y
        h = modulate(rms_norm(x, norm_ffn_g[i]), sh2, sc2)
        x = x + g2 * swiglu_ffn(h, ffn_w_in[i], ffn_w_out[i])
    return rms_norm(x, final_g)


_drawn_inputs = setup_inputs


def setup_inputs(seed=0):
    import zlib

    import numpy as np

    out = dict(_drawn_inputs(seed))
    spreads = {}
    factors = {'norm_ffn_g': 2.885, 'norm_mix_g': 3.16, 'final_g': 2.779}
    for name, (base, spread) in spreads.items():
        noise = np.random.default_rng([zlib.crc32(name.encode()), seed]).standard_normal(out[name].shape)
        drawn = base * np.exp(spread * noise) if base else spread * noise
        out[name] = __import__('jax').numpy.asarray(drawn.astype(out[name].dtype))
    for name, factor in factors.items():
        out[name] = (out[name] * factor).astype(out[name].dtype)
    return out
```

```python
from contextlib import ExitStack

import numpy as np

import concourse.bass as bass
from concourse import mybir

F32 = mybir.dt.float32
F32R = mybir.dt.float32r
ALU = mybir.AluOpType
ACT = mybir.ActivationFunctionType
AX_X = mybir.AxisListType.X

P = 128
D = 1024
S = 512
KT = D // P
F = 2816
FT = F // P
FH = FT // 2
DH = 64
GROUPS = 3
CLS = 4
EPS = 1e-6
SCALE = DH ** -0.5
NEG = -1e30
WIN = DH
WSTART = (0, 16, 48, 64)
HEAD_PAIRS = 4

BLOCKS = 8
SLAB = BLOCKS * P
RING = 3
HALF_SLABS = 36
WO0 = 2 * HALF_SLABS
FFN0 = WO0 + KT
FFN_SLABS = 2 * (2 * FH + FH)
CONV_IN = FFN0 + FFN_SLABS
CONV_OUT = CONV_IN + 3 * KT
FFN1 = CONV_OUT + KT
SLABS = FFN1 + FFN_SLABS

AJ = 512
ARING = 4
JOBS_START = 4
JOBS_L0 = 12
JOBS = 24
TILE_UNIT = {0: 0, 1: 1, 2: 2, 4: 3, 5: 4, 6: 5}
UNITS = 4 * 2 * CLS
FFO_SLAB = tuple((FH * m + FH - 1) // BLOCKS for m in range(KT))
V_BANK = ((0, 1, 2, 3), (4, 5, 0, 1), (2, 3, 4, 5))
CHUNKS_PAIR = ((0, 1), (2,), (3,), (4, 5), (6,), (7,))
CHUNKS_FFN = tuple(tuple(divmod(c, 8) for c in range(a, b)) for a, b in ((0, 6), (6, 11), (11, 16)))
LINKS_PAIR = 23
FFO_BANK = (0, 1, 2, 3, 4, 5, 4, 5)
HID_O, HID_F0, HID_CONV, HID_F1 = 0, KT, KT + 2 * FH, 2 * KT + 2 * FH
SH1, SC1, G1, SH2, SC2, G2 = (KT * n for n in range(6))
L1 = 6 * KT


def encoder(nc, xT, cT, wstream, adaw, adab, gains, convw, masks, rope, ident, outT):
    with ExitStack() as ctx:
        start = nc.sbuf_base
        at = [(start + 63) // 64 * 64]

        def sb(name, shape, dt=F32):
            t = nc.alloc_sbuf_tensor_at(name, shape, dt, offset=at[0])
            at[0] += (4 * int(np.prod(shape[1:])) + 63) // 64 * 64
            return t

        def sem(name):
            return ctx.enter_context(nc.semaphore(name))

        x = sb("x", [P, KT, S])
        hh = sb("h_hi", [P, KT, S], F32R)
        hl = sb("h_lo", [P, KT, S], F32R)
        raw = sb("w_raw", [P, RING, SLAB])
        whi = sb("w_hi", [P, RING, SLAB], F32R)
        wlo = sb("w_lo", [P, RING, SLAB], F32R)
        aring = sb("ada_ring", [P, ARING, AJ])
        acc = sb("ada_acc", [P, 2, AJ])
        modv = sb("mod", [P, 12 * KT])
        bias = sb("ada_bias", [P, 12 * KT])
        cond = sb("cond", [P, KT])
        gain = sb("gains", [P, 5 * KT])
        aff = sb("mod_gain", [P, 4 * KT])
        cw = sb("conv_w", [P, 3 * KT])
        ones = sb("ones", [P, P])
        idn = sb("ident", [P, P])
        var = sb("variance", [P, CLS])
        rstd = sb("rstd", [P, CLS])
        region = at[0]
        cosT = sb("cos", [P, S])
        sinT = sb("sin", [P, S])
        mask = sb("mask", [P, CLS, S + 2 * P])
        V = sb("v", [P, GROUPS, CLS, S])
        q0 = {(e, a, b): sb(f"q0_{e}{a}{b}", [P, S], F32R) for e in (0, 1) for a in ("hi", "lo") for b in (0, 1)}
        k0h = [sb(f"k0_hi{e}", [P, S], F32R) for e in (0, 1)]
        k0l = [sb(f"k0_lo{e}", [P, S], F32R) for e in (0, 1)]
        qg = {(e, g, b): sb(f"q{g}_{e}{b}", [P, S]) for e in (0, 1) for g in (1, 2) for b in (0, 1)}
        kg = {(e, g): sb(f"k{g}_{e}", [P, S]) for e in (0, 1) for g in (1, 2)}
        ropeA = sb("rope_a", [P, S])
        ropeB = sb("rope_b", [P, S])
        Sb = sb("probs", [P, 2, S + 2 * P])
        nmax = sb("neg_max", [P, 4])
        turn = sb("turn", [P, 4])
        den = sb("denom", [P, 4])
        rden = sb("denom_inv", [P, 4])
        PT0 = sb("probs_t0", [P, CLS, CLS, WIN])
        PT12 = sb("probs_t12", [P, 2, CLS, P])
        assert at[0] <= nc.sbuf_usable_end, at[0]
        at[0] = region
        hidh = sb("hid_hi", [P, FH, S], F32R)
        hidl = sb("hid_lo", [P, FH, S], F32R)
        gate = sb("gate", [P, 3, S])
        cbuf = sb("conv_c", [P, 2, S])
        cu = sb("conv_cu", [P, S + 2])
        zb = sb("conv_z", [P, S])
        sq = sb("squares", [P, KT, S])
        ssum = sb("square_sum", [P, S])
        xr = sb("x_rstd", [P, 2, S])
        diag = sb("rstd_diag", [P, CLS, P])
        assert at[0] <= nc.sbuf_usable_end, at[0]

        ps = ctx.enter_context(nc.psum_tensor("ps", [P, 8, 512], F32))
        flat = ps[:, :, :].rearrange("p b n -> p (b n)")
        MODB = 7
        SBANK, PTB, OB = 2, 4, 6
        NB = 6

        raw_in = [sem(f"raw_in{i}") for i in range(RING)]
        hi_ready = sem("hi_ready")
        lo_ready = sem("lo_ready")
        slab_done = sem("slab_done")
        ada_in = [sem(f"ada_in{i}") for i in range(ARING)]
        ada_acc = sem("ada_acc")
        ada_red = sem("ada_red")
        small_in = sem("small_in")
        tables_in = sem("tables_in")
        id_in = sem("id_in")
        x_in = sem("x_in")
        cond_ready = sem("cond_ready")
        setup = sem("setup")
        sq_ready = sem("sq_ready")
        ssum_ready = sem("ssum_ready")
        ssq_ready = sem("ssq_ready")
        var_ready = sem("var_ready")
        rstd_ready = sem("rstd_ready")
        xr_ready = sem("xr_ready")
        diag_ready = sem("diag_ready")
        rb_ready = sem("rb_ready")
        part_sum = sem("part_sum")
        hhi_ready = sem("hhi_ready")
        h_ready = sem("h_ready")
        v_done = sem("v_done")
        v_act = sem("v_act")
        v_dve = sem("v_dve")
        rope_raw = sem("rope_raw")
        rope_read = sem("rope_read")
        q0_hi = sem("q0_hi")
        qk_ready = sem("qk_ready")
        s_done = sem("s_done")
        s_read = sem("s_read")
        exp_done = sem("exp_done")
        prob_ready = sem("prob_ready")
        pt_done = sem("pt_done")
        pt0_ready = sem("pt0_ready")
        pt12_ready = sem("pt12_ready")
        pv_done = sem("pv_done")
        o_ready = sem("o_ready")
        x_upd = sem("x_upd")
        ffo_done = sem("ffo_done")
        gate_ready = sem("gate_ready")
        hid_hi = sem("hid_hi_ready")
        hid_lo = sem("hid_lo_ready")
        cpy_ready = sem("cpy_ready")
        y_raw = sem("y_raw")
        link_dve = sem("link_dve")
        link_cos = sem("link_cos")
        fin_ready = sem("fin_ready")
        out_done = sem("out_done")

        def wblk(t, slot, b, n=P):
            return t[:, slot, b * P:b * P + n]

        def classes(ap):
            return ap.rearrange("p (m r) -> p r m", r=CLS)

        U_WO, U_F0, U_CO = KT, 3 * KT, 4 * KT

        block = ctx.enter_context(nc.Block())

        @block.sync
        def _(sp):
            def load_slab(q, c):
                n = 3 * q + c
                if not (isinstance(n, int) and n < RING):
                    sp.wait_ge(lo_ready, n - 2)
                sp.dma_start(raw[:, c % RING, :], wstream[n]).then_inc(raw_in[c % RING], 16)

            def load_ada(job, k):
                if not (isinstance(job, int) and job == 0 and k < ARING):
                    sp.wait_ge(ada_acc, 8 * job + k - 3)
                sp.dma_start(aring[:, k % ARING, :], adaw[job, k]).then_inc(ada_in[k % ARING], 16)

            sp.dma_start(cond[:, :], cT).then_inc(small_in, 16)
            sp.dma_start(bias[:, :], adab).then_inc(small_in, 16)
            sp.dma_start(gain[:, :], gains).then_inc(small_in, 16)
            for job in range(JOBS_START):
                for k in range(8):
                    load_ada(job, k)
                    if job < 2 and k % 2:
                        t = 4 * job + k // 2
                        sp.dma_start(x[:, t, :], xT[:, t, :]).then_inc(x_in, 16)
                if job == 0:
                    sp.dma_start(idn[:, :], ident).then_inc(id_in, 16)
                if job == 1:
                    for n in range(RING):
                        load_slab(0, n)
            sp.dma_start(cw[:, :], convw).then_inc(tables_in, 16)
            sp.dma_start(cosT[:, :], rope[0]).then_inc(tables_in, 16)
            sp.dma_start(sinT[:, :], rope[1]).then_inc(tables_in, 16)
            sp.dma_start(mask[:, :, :], masks).then_inc(tables_in, 16)
            with sp.Fori(0, 2) as hf:
                with sp.Fori(0, 4) as i:
                    for c in range(3):
                        load_slab(hf * 12 + i + 1, c)
                with sp.Fori(0, 4) as pr:
                    for c in range(6):
                        for k in CHUNKS_PAIR[c]:
                            load_ada(JOBS_START + hf * 4 + pr, k)
                        load_slab(hf * 12 + pr * 2 + 5, c)
            sp.wait_ge(hid_lo, KT)
            sp.dma_start(x[:, :, :], xT).then_inc(x_in, 16)
            for m in range(KT):
                load_slab(WO0 // 3 + 1, m)
            for half in range(2):
                n0 = FFN0 + half * 3 * FH + RING
                with sp.Fori(0, 3) as i:
                    for t in range(3):
                        for jj, k in CHUNKS_FFN[t]:
                            load_ada(JOBS_L0 + half * 6 + i * 2 + jj, k)
                        for s in range(2):
                            load_slab(i * 2 + n0 // 3, n0 % 3 + 2 * t + s)
                n1 = n0 + 18
                with sp.Fori(0, 5) as i:
                    for c in range(3):
                        load_slab(i + n1 // 3, n1 % 3 + c)
            n0 = CONV_IN + RING
            trips, rest = divmod(SLABS - n0, 3)
            with sp.Fori(0, trips) as i:
                for c in range(3):
                    load_slab(i + n0 // 3, n0 % 3 + c)
            for c in range(rest):
                load_slab(trips + n0 // 3, n0 % 3 + c)
            for t in range(KT):
                sp.wait_ge(fin_ready, t + 1)
                sp.dma_start(outT[:, t, :], sq[:, t, :]).then_inc(out_done, 16)
            sp.wait_ge(out_done, 16 * KT)

        @block.gpsimd
        def _(pool):
            def low(q, c):
                n = 3 * q + c
                pool.wait_ge(hi_ready, n + 1)
                s = c % RING
                nc.gpsimd.tensor_tensor(wlo[:, s, :], raw[:, s, :], whi[:, s, :].bitcast(F32),
                                        ALU.subtract).then_inc(lo_ready, 1)

            for t in range(1, KT):
                pool.wait_ge(sq_ready, t + 1)
                if t > 1:
                    pool.wait_ge(part_sum, t - 1)
                ins = nc.gpsimd.tensor_tensor(ssum[:, :], sq[:, 0, :] if t == 1 else ssum[:, :], sq[:, t, :], ALU.add)
                ins.then_inc(part_sum if t < KT - 1 else ssum_ready, 1)
            trips, rest = divmod(SLABS, 3)
            with pool.Fori(0, trips) as i:
                for c in range(3):
                    low(i, c)
            for c in range(rest):
                low(trips, c)

        @block.scalar
        def _(act):
            def high(q, c):
                n = 3 * q + c
                if isinstance(n, int):
                    if n >= SLABS:
                        return
                    if n >= RING:
                        act.wait_ge(slab_done, n - 2)
                else:
                    act.wait_ge(slab_done, n - 2)
                act.wait_ge(raw_in[c % RING], (q + c // RING) * 16 + 16)
                nc.scalar.copy(whi[:, c % RING, :], raw[:, c % RING, :]).then_inc(hi_ready, 1)

            def square(i, t, upd):
                if upd is None:
                    act.wait_ge(x_in, 16 * KT)
                else:
                    act.wait_ge(x_upd, upd + t + 1)
                nc.scalar.activation(sq[:, t, :], x[:, t, :], ACT.Square).then_inc(sq_ready, 1)

            def norm_out(i, vec):
                act.wait_ge(var_ready, i + 1)
                nc.scalar.activation(rstd[:, :], var[:, :], ACT.Sqrt).then_inc(rstd_ready, 1)
                if vec is None:
                    return
                for t in range(KT):
                    act.wait_ge(xr_ready, i * KT + t + 1)
                    nc.scalar.activation(hh[:, t, :], xr[:, t % 2, :], ACT.Identity,
                                         bias=modv[:, vec + t:vec + t + 1]).then_inc(hhi_ready, 1)

            act.wait_ge(small_in, 48)
            nc.scalar.activation(cond[:, :], cond[:, :], ACT.Silu).then_inc(cond_ready, 1)
            for t in range(KT):
                square(0, t, None)
            for n in range(RING):
                high(0, n)
            norm_out(0, SH1)
            with act.Fori(0, 2) as hf:
                for g in range(GROUPS):
                    for s in range(4):
                        high(hf * 12, 4 * g + s + RING)
                    for tt in (0, 1):
                        act.wait_ge(v_done, hf * 9 + 3 * g + tt + 1)
                        nc.scalar.copy(V[:, g, tt, :], ps[:, V_BANK[g][tt], :]).then_inc(v_act, 1)

                def tile_parts(pr, i):
                    e = pr % 2
                    if i < 2:
                        act.wait_ge(rope_raw, hf * 8 + 2 * pr + i + 1)
                    if i == 0:
                        for b in (0, 1):
                            r = slice(DH * b, DH * b + DH)
                            nc.scalar.copy(q0[e, "hi", b][r, :].rearrange("p (r m) -> p r m", r=CLS),
                                           classes(ropeA[r, :])).then_inc(q0_hi, 1)
                    if i == 1:
                        nc.scalar.copy(k0h[e][:, :], ropeA[:, :]).then_inc(q0_hi, 1)

                def probs(u):
                    n = hf * UNITS + u
                    act.wait_ge(s_read, n + 1)
                    nc.scalar.activation(Sb[:, u % 2, :], Sb[:, u % 2, :], ACT.Exp,
                                         bias=nmax[:, u % 4:u % 4 + 1], scale=-1.0,
                                         accum_out=den[:, u % 4:u % 4 + 1]).then_inc(exp_done, 1)

                def take_t(u):
                    if u % 4 == 0 and u:
                        act.wait_ge(pv_done, hf * 8 + u // 4)
                    act.wait_ge(pt_done, hf * UNITS + u + 1)
                    for h2 in (0, 1):
                        o = PTB * 512 + 304 * h2
                        src = flat[:, o:o + 288].rearrange("p (t n) -> p t n", t=2)[:, :, 0:WIN]
                        nc.scalar.copy(PT0[:, 2 * h2:2 * h2 + 2, u % 4, :], src).then_inc(pt0_ready, 1)

                def take_o(pr):
                    act.wait_ge(pv_done, hf * 8 + (2 * pr + 2))
                    nc.scalar.copy(x[:, bass.ds(hf * 4 + pr, 1), :].rearrange("p a (m r) -> p (a r) m", r=CLS),
                                   ps[:, OB, :].rearrange("p (r m) -> p r m", r=CLS)).then_inc(o_ready, 1)

                for i in range(6):
                    high(hf * 12, 12 + i + RING)
                    tile_parts(0, i)
                for u in range(UNITS + 1):
                    pr, i = u // 8 + 1, TILE_UNIT.get(u % 8)
                    tile = i is not None and pr < HEAD_PAIRS
                    if u < UNITS:
                        probs(u)
                    if tile:
                        high(hf * 12, 12 + 6 * pr + i + RING)
                    if u:
                        take_t(u - 1)
                    if tile:
                        tile_parts(pr, i)
                    if u % 8 == 1 and u > 8:
                        take_o(u // 8 - 1)
                take_o(HEAD_PAIRS - 1)
            for t in range(KT):
                act.wait_ge(o_ready, t + 1)
                nc.scalar.copy(hh[:, t, :], x[:, t, :]).then_inc(hid_hi, 1)
            for m in range(KT):
                high(WO0 // 3, m + RING)
                square(1, m, 0)

            def ffn(i, base, upd):
                norm_out(i, SH2 if i == 1 else L1 + SH2)
                for half in range(2):
                    n0 = base + half * 3 * FH

                    def gated(slabs, t):
                        act.wait_ge(slab_done, slabs)
                        nc.scalar.activation(gate[:, t % 3, :], ps[:, 2 * (t % 3), :],
                                             ACT.Silu).then_inc(gate_ready, 1)

                    with act.Fori(0, 3) as it:
                        for t in range(3):
                            gated(it * 6 + (n0 + 2 * t + 1), t)
                            for s in range(2):
                                high(it * 2 + n0 // 3, n0 % 3 + 2 * t + s + RING)
                    for t in range(9, FH):
                        gated(n0 + 2 * t + 1, t)
                        for s in range(2):
                            high(0, n0 + 2 * t + s + RING)
                    for s in range(FH):
                        high(0, n0 + 2 * FH + s + RING)
                        if half and s in FFO_SLAB:
                            square(i + 1, FFO_SLAB.index(s), upd + KT)

            ffn(1, FFN0, U_WO)
            norm_out(2, L1 + SH1)
            with act.Fori(0, KT // 2) as it:
                for t in range(2):
                    for s in range(3):
                        high(it * 2 + CONV_IN // 3, CONV_IN % 3 + 3 * t + s + RING)
                    act.wait_ge(slab_done, it * 6 + (CONV_IN + 3 * t + 2))
                    nc.scalar.copy(cbuf[:, t, :], ps[:, 3 * t + 1, :]).then_inc(cpy_ready, 1)
            for m in range(KT):
                high(0, CONV_OUT + m + RING)
                square(3, m, U_F0)
            ffn(3, FFN1, U_CO)
            norm_out(4, None)

        @block.vector
        def _(dve):
            step = {"base": 0, "n": 0}

            def link(ins):
                step["n"] += 1
                ins.then_inc(link_dve, 1)
                dve.wait_ge(link_dve, step["base"] + step["n"])

            def enter(reg, per):
                step["saved"] = step["base"] + step["n"]
                step["base"], step["n"], step["per"] = reg * per + step["saved"], 0, per

            def leave(trips):
                assert step["n"] == step["per"], step
                step["base"], step["n"] = step["saved"] + trips * step["per"], 0

            def ada_chunk(job, k, par):
                dve.wait_ge(ada_in[k % ARING], job * 32 + 16 * (k // ARING) + 16)
                src = aring[:, k % ARING, :]
                if k == 0:
                    if not (isinstance(job, int) and job < 2):
                        dve.wait_ge(ada_red, job - 1)
                    nc.vector.tensor_scalar(acc[:, par, :], src, cond[:, 0:1], None, ALU.mult).then_inc(ada_acc, 1)
                else:
                    dve.wait_ge(ada_acc, job * 8 + k)
                    nc.vector.scalar_tensor_tensor(out=acc[:, par, :], in0=src, scalar=cond[:, k:k + 1],
                                                   in1=acc[:, par, :],
                                                   op0=ALU.mult, op1=ALU.add).then_inc(ada_acc, 1)

            def mod_add(job, jobs):
                dve.wait_ge(ada_red, job + jobs)
                c = bass.ds(job * 4, 4 * jobs)
                link(nc.vector.tensor_tensor(modv[:, c], ps[:, MODB, c], bias[:, c], ALU.add))

            def add_square(i, t):
                dve.wait_ge(sq_ready, i * KT + t + 1)
                if t == 1:
                    link(nc.vector.tensor_tensor(ssum[:, :], sq[:, 0, :], sq[:, 1, :], ALU.add))
                elif 1 < t < KT - 1:
                    link(nc.vector.tensor_tensor(ssum[:, :], ssum[:, :], sq[:, t, :], ALU.add))
                elif t == KT - 1:
                    nc.vector.tensor_tensor(ssum[:, :], ssum[:, :], sq[:, t, :], ALU.add).then_inc(ssum_ready, 1)

            def norm(i, vec):
                if vec is not None:
                    a = slice(KT * i, KT * i + KT)
                    sc = slice(vec, vec + KT)
                    link(nc.vector.scalar_tensor_tensor(out=aff[:, a], in0=modv[:, sc], scalar=1.0,
                                                        in1=gain[:, KT * i:KT * i + KT],
                                                        op0=ALU.add, op1=ALU.mult))
                dve.wait_ge(ssq_ready, i + 1)
                link(nc.vector.tensor_scalar(var[:, :], ps[:, NB, 0:CLS], 1.0 / D, EPS, ALU.mult, ALU.add))
                nc.vector.reciprocal(var[:, :], var[:, :]).then_inc(var_ready, 1)
                dve.wait_ge(rstd_ready, i + 1)
                for t in range(CLS):
                    nc.vector.tensor_scalar(diag[:, t, :], idn[:, :], rstd[:, t:t + 1], None,
                                            ALU.mult).then_inc(diag_ready, 1)
                dve.wait_ge(rb_ready, i + 1)
                for t in range(KT):
                    if vec is None:
                        nc.vector.scalar_tensor_tensor(out=sq[:, t, :], in0=x[:, t, :],
                                                       scalar=gain[:, KT * i + t:KT * i + t + 1],
                                                       in1=ps[:, NB, :], op0=ALU.mult,
                                                       op1=ALU.mult).then_inc(fin_ready, 1)
                        continue
                    if i * KT + t >= 2:
                        dve.wait_ge(h_ready, i * KT + t - 1)
                    nc.vector.scalar_tensor_tensor(out=xr[:, t % 2, :], in0=x[:, t, :],
                                                   scalar=aff[:, KT * i + t:KT * i + t + 1], in1=ps[:, NB, :],
                                                   op0=ALU.mult, op1=ALU.mult).then_inc(xr_ready, 1)
                    if t:
                        low_h(i, t - 1, vec - KT)
                if vec is not None:
                    low_h(i, KT - 1, vec - KT)

            def low_h(i, t, vec):
                dve.wait_ge(hhi_ready, i * KT + t + 1)
                nc.vector.scalar_tensor_tensor(out=hl[:, t, :], in0=xr[:, t % 2, :], scalar=modv[:, vec + t:vec + t + 1],
                                               in1=hh[:, t, :].bitcast(F32), op0=ALU.add,
                                               op1=ALU.subtract).then_inc(h_ready, 1)

            nc.vector.memset(ones[:, :], 1.0).then_inc(setup, 1)
            dve.wait_ge(cond_ready, 1)
            for job in range(JOBS_START):
                for k in range(8):
                    ada_chunk(job, k, job % 2)
            mod_add(0, JOBS_START)
            dve.wait_ge(id_in, 16)
            norm(0, SC1)
            dve.wait_ge(h_ready, KT)
            for e in (0, 1):
                for b in (0, 1):
                    r = slice(DH * (1 - b), DH * (1 - b) + DH)
                    for a in ("hi", "lo"):
                        nc.vector.memset(q0[e, a, b][r, :].bitcast(F32), 0.0).then_inc(setup, 1)
                    for g in (1, 2):
                        nc.vector.memset(qg[e, g, b][r, :], 0.0).then_inc(setup, 1)

            swap = [(j + 8) % 16 if j < 16 else j for j in range(32)]
            with dve.Fori(0, 2) as hf:
                enter(hf, HEAD_PAIRS * LINKS_PAIR)
                for g in range(GROUPS):
                    for tt in (2, 3):
                        if tt == 2:
                            dve.wait_ge(v_done, hf * 9 + 3 * g + 3)
                        else:
                            dve.wait_ge(slab_done, hf * HALF_SLABS + 4 * g + 4)
                        nc.vector.tensor_copy(V[:, g, tt, :], ps[:, V_BANK[g][tt], :]).then_inc(v_dve, 1)

                def chunks(pr, i):
                    for k in CHUNKS_PAIR[i]:
                        ada_chunk(hf * 4 + (JOBS_START + pr), k, pr % 2)

                def rotate(pr, i):
                    g, is_k, e = i // 2, i % 2, pr % 2
                    dve.wait_ge(slab_done, hf * HALF_SLABS + (12 + 6 * pr + i + 1))
                    if i == 1 or i == 2:
                        dve.wait_ge(q0_hi, hf * 12 + (3 * pr + (2 if i == 1 else 3)))
                    if pr == 0 and i == 0:
                        dve.wait_ge(tables_in, 64)
                    nc.vector.tensor_tensor(ropeA[:, :], ps[:, i % 2, :], cosT[:, :],
                                            ALU.mult).then_inc(link_cos, 1)
                    nc.vector.stream_shuffle(ropeB[:, :], ps[:, i % 2, :], swap).then_inc(rope_read, 1)
                    dve.wait_ge(rope_read, hf * 24 + (6 * pr + i + 1))
                    link(nc.vector.tensor_tensor(ropeB[:, :], ropeB[:, :], sinT[:, :], ALU.mult))
                    dve.wait_ge(link_cos, hf * 24 + (6 * pr + i + 1))
                    if g == 0:
                        nc.vector.tensor_tensor(ropeA[:, :], ropeA[:, :], ropeB[:, :],
                                                ALU.add).then_inc(rope_raw, 1)
                        if is_k:
                            dve.wait_ge(q0_hi, hf * 12 + (3 * pr + 3))
                            link(nc.vector.tensor_tensor(k0l[e][:, :], ropeA[:, :], k0h[e][:, :].bitcast(F32),
                                                         ALU.subtract))
                        else:
                            for b in (0, 1):
                                r = slice(DH * b, DH * b + DH)
                                dve.wait_ge(q0_hi, hf * 12 + (3 * pr + b + 1))
                                link(nc.vector.tensor_tensor(
                                    q0[e, "lo", b][r, :].rearrange("p (r m) -> p r m", r=CLS),
                                    classes(ropeA[r, :]),
                                    q0[e, "hi", b][r, :].bitcast(F32).rearrange("p (r m) -> p r m", r=CLS),
                                    ALU.subtract))
                    elif is_k:
                        ins = nc.vector.tensor_tensor(kg[e, g][:, :].rearrange("p (r m) -> p r m", r=CLS),
                                                      classes(ropeA[:, :]), classes(ropeB[:, :]), ALU.add)
                        if g == 2:
                            ins.then_inc(qk_ready, 1)
                        else:
                            link(ins)
                    else:
                        for b in (0, 1):
                            r = slice(DH * b, DH * b + DH)
                            link(nc.vector.tensor_tensor(
                                qg[e, g, b][r, :].rearrange("p (r m) -> p r m", r=CLS),
                                classes(ropeA[r, :]), classes(ropeB[r, :]), ALU.add))

                def masked(u):
                    dve.wait_ge(s_done, hf * UNITS + (u + 1))
                    nc.vector.memset(turn[:, u % 4:u % 4 + 1], 0.0)
                    nc.vector.tensor_tensor_reduce(
                        Sb[:, u % 2, :], flat[:, SBANK * 512:SBANK * 512 + 768], mask[:, u % 4, :],
                        -SCALE, 3e38, ALU.add, ALU.min, nmax[:, u % 4:u % 4 + 1]).then_inc(s_read, 1)

                def normalise(u):
                    dve.wait_ge(exp_done, hf * UNITS + (u + 1))
                    link(nc.vector.reciprocal(rden[:, u % 4:u % 4 + 1], den[:, u % 4:u % 4 + 1]))
                    nc.vector.tensor_scalar(Sb[:, u % 2, :], Sb[:, u % 2, :], rden[:, u % 4:u % 4 + 1],
                                            None, ALU.mult).then_inc(prob_ready, 1)

                def take_t(u):
                    if u % 4 == 0 and u:
                        dve.wait_ge(pv_done, hf * 8 + u // 4)
                    dve.wait_ge(pt_done, hf * UNITS + (u + 1))
                    nc.vector.tensor_copy(PT12[:, :, u % 4, :],
                                          ps[:, PTB + 1, 0:256].rearrange("p (g n) -> p g n", g=2)
                                          ).then_inc(pt12_ready, 1)

                for i in range(6):
                    chunks(0, i)
                    rotate(0, i)
                mod_add(hf * 4 + JOBS_START, 1)
                for u in range(UNITS + 1):
                    pr, i = u // 8 + 1, TILE_UNIT.get(u % 8)
                    tile = i is not None and pr < HEAD_PAIRS
                    if u < UNITS:
                        masked(u)
                    if tile:
                        chunks(pr, i)
                    if u < UNITS:
                        normalise(u)
                    if u:
                        take_t(u - 1)
                    if tile:
                        rotate(pr, i)
                    if u % 8 == 7 and pr < HEAD_PAIRS:
                        mod_add(hf * 4 + (JOBS_START + pr), 1)
                leave(2)

            for t in range(KT):
                dve.wait_ge(hid_hi, t + 1)
                nc.vector.tensor_tensor(hl[:, t, :], x[:, t, :], hh[:, t, :].bitcast(F32),
                                        ALU.subtract).then_inc(hid_lo, 1)

            def residual(src, gvec, m):
                nc.vector.scalar_tensor_tensor(out=x[:, m, :], in0=src, scalar=modv[:, gvec + m:gvec + m + 1],
                                               in1=x[:, m, :], op0=ALU.mult, op1=ALU.add).then_inc(x_upd, 1)

            for m in range(KT):
                dve.wait_ge(slab_done, WO0 + m + 1)
                if m == 0:
                    dve.wait_ge(x_in, 16 * (KT + 1))
                residual(ps[:, m % 2, :], G1, m)
                if m:
                    add_square(1, m - 1)
            add_square(1, KT - 1)

            def ffn(i, base, layer, upd):
                norm(i, layer * L1 + SC2)
                for half in range(2):
                    n0 = base + half * 3 * FH
                    g0 = (HID_F1 if layer else HID_F0) + half * FH
                    gates = (2 * layer + half) * FH

                    def hidden(slabs, cnt, t, dst):
                        dve.wait_ge(slab_done, slabs)
                        dve.wait_ge(gate_ready, dst + (gates + 1))
                        gt = gate[:, t % 3, :]
                        link(nc.vector.tensor_tensor(gt, gt, ps[:, 2 * (t % 3) + 1, :], ALU.mult))
                        hi = hidh[:, bass.ds(dst, 1), :].rearrange("p a n -> p (a n)")
                        lo = hidl[:, bass.ds(dst, 1), :].rearrange("p a n -> p (a n)")
                        nc.vector.tensor_copy(hi, gt).then_inc(hid_hi, 1)
                        dve.wait_ge(hid_hi, cnt + 1)
                        nc.vector.tensor_tensor(lo, gt, hi.bitcast(F32), ALU.subtract).then_inc(hid_lo, 1)

                    with dve.Fori(0, 3) as it:
                        enter(it, 3 + (layer == 0))
                        job = it * 2 + (JOBS_L0 + half * 6)
                        for t in range(3):
                            if layer == 0:
                                for jj, k in CHUNKS_FFN[t]:
                                    ada_chunk(job + jj, k, jj)
                            hidden(it * 6 + (n0 + 2 * t + 2), it * 3 + (g0 + t), t, it * 3 + t)
                        if layer == 0:
                            mod_add(job, 2)
                        leave(3)
                    for t in range(9, FH):
                        hidden(n0 + 2 * t + 2, g0 + t, t, t)
                    for m in range(KT):
                        if m < KT - 1:
                            dve.wait_ge(ffo_done, (2 * layer + half) * (KT - 1) + m + 1)
                        else:
                            dve.wait_ge(slab_done, n0 + 3 * FH)
                        if half:
                            dve.wait_ge(x_upd, upd + m + 1)
                        residual(ps[:, FFO_BANK[m], :], layer * L1 + G2, m)
                        if half and m:
                            add_square(i + 1, m - 1)
                add_square(i + 1, KT - 1)

            ffn(1, FFN0, 0, U_WO)
            norm(2, L1 + SC1)
            link(nc.vector.memset(cu[:, :], 0.0))
            with dve.Fori(0, KT // 2) as it:
                enter(it, 2 * 4)
                for t in range(2):
                    m = it * 2 + t
                    dve.wait_ge(slab_done, it * 6 + (CONV_IN + 3 * t + 3))
                    dve.wait_ge(cpy_ready, m + 1)
                    link(nc.vector.tensor_tensor(cu[:, 1:S + 1], cbuf[:, t, :], ps[:, 3 * t + 2, :], ALU.mult))
                    link(nc.vector.tensor_scalar(zb[:, :], cu[:, 0:S], cw[:, bass.ds(m * 3, 1)], None, ALU.mult))
                    for w in (1, 2):
                        link(nc.vector.scalar_tensor_tensor(out=zb[:, :], in0=cu[:, w:S + w],
                                                            scalar=cw[:, bass.ds(m * 3 + w, 1)], in1=zb[:, :],
                                                            op0=ALU.mult, op1=ALU.add))
                    nc.vector.tensor_tensor(zb[:, :], zb[:, :], ps[:, 3 * t, :], ALU.mult).then_inc(y_raw, 1)
                    dve.wait_ge(y_raw, m + 1)
                    hi = hidh[:, bass.ds(m, 1), :].rearrange("p a n -> p (a n)")
                    lo = hidl[:, bass.ds(m, 1), :].rearrange("p a n -> p (a n)")
                    nc.vector.tensor_copy(hi, zb[:, :]).then_inc(hid_hi, 1)
                    dve.wait_ge(hid_hi, m + (HID_CONV + 1))
                    nc.vector.tensor_tensor(lo, zb[:, :], hi.bitcast(F32), ALU.subtract).then_inc(hid_lo, 1)
                leave(KT // 2)
            for m in range(KT):
                dve.wait_ge(slab_done, CONV_OUT + m + 1)
                residual(ps[:, m % 2, :], L1 + G1, m)
                if m:
                    add_square(3, m - 1)
            add_square(3, KT - 1)
            ffn(3, FFN1, 1, U_CO)
            norm(4, None)

        @block.tensor
        def _(pe):
            def passes(out, w_hi, w_lo, a_hi, a_lo, first, last):
                nc.tensor.matmul(out, w_hi, a_hi, start=first, stop=False)
                nc.tensor.matmul(out, w_hi, a_lo, start=False, stop=False)
                return nc.tensor.matmul(out, w_lo, a_hi, start=False, stop=last)

            def slab(q, c):
                pe.wait_ge(lo_ready, 3 * q + c + 1)
                return c % RING

            def project(q, c, bank, ah=hh, al=hl, tiles=None):
                s = slab(q, c)
                for k in range(KT):
                    if tiles is not None:
                        pe.wait_ge(tiles[0], tiles[1] + k + 1)
                    last = passes(ps[:, bank, :], wblk(whi, s, k), wblk(wlo, s, k), ah[:, k, :], al[:, k, :],
                                  k == 0, k == KT - 1)
                last.then_inc(slab_done, 1)

            def reduce_ada(job, par):
                pe.wait_ge(ada_acc, job * 8 + 8)
                for c in range(AJ // P):
                    last = nc.tensor.matmul(ps[:, MODB, bass.ds(job * 4 + c, 1)], acc[:, par, c * P:c * P + P],
                                            ones[:, 0:1], start=True, stop=True)
                last.then_inc(ada_red, 1)

            def mean_square(i):
                pe.wait_ge(ssum_ready, i + 1)
                for t in range(CLS):
                    last = nc.tensor.matmul(ps[:, NB, t:t + 1], ssum[:, t * P:t * P + P], ones[:, 0:1],
                                            start=True, stop=True)
                last.then_inc(ssq_ready, 1)
                pe.wait_ge(diag_ready, CLS * (i + 1))
                nc.tensor.matmul(ps[:, NB, :], ones[:, :], diag[:, :, :].rearrange("p t n -> p (t n)"),
                                 start=True, stop=True).then_inc(rb_ready, 1)

            def values(hf, n):
                pr, head = divmod(n, 2)
                units = hf * UNITS + (4 * n + 4)
                pe.wait_ge(pt0_ready, units * 2)
                pe.wait_ge(pt12_ready, units)
                if head == 0 and pr:
                    pe.wait_ge(o_ready, hf * 4 + pr)
                rows = slice(DH * head, DH * head + DH)
                cols = slice(pr * P + DH * head, pr * P + DH * head + DH)
                for g in (1, 2):
                    for r in range(CLS):
                        nc.tensor.matmul(ps[rows, OB, r * P:r * P + P], V[:, g, r, cols], PT12[:, g - 1, r, :],
                                         start=(g == 1 and r == 0), stop=False)
                out = ps[rows, OB, :].rearrange("p (r m) -> p r m", r=CLS)
                for t in range(CLS):
                    last = nc.tensor.matmul(out[:, :, WSTART[t]:WSTART[t] + WIN], V[:, 0, t, cols], PT0[:, t, :, :],
                                            start=False, stop=(t == CLS - 1))
                last.then_inc(pv_done, 1)

            pe.wait_ge(setup, 1)
            for job in range(JOBS_START):
                reduce_ada(job, job % 2)
            mean_square(0)
            with pe.Fori(0, 2) as hf:
                for g in range(GROUPS):
                    for s in range(4):
                        sl = slab(hf * 12, 4 * g + s)
                        for tt in range(CLS):
                            if s == 0 and (g == 2 or (g == 1 and tt > 1)):
                                copied, n = (v_act, 2 * g + tt - 3) if tt > 1 else (v_dve, tt + 1)
                                pe.wait_ge(copied, hf * 6 + n)
                            for kk in range(2):
                                k = 2 * s + kk
                                if g == 0 and tt == 0:
                                    pe.wait_ge(h_ready, k + 1)
                                tok = slice(tt * P, tt * P + P) if g == 0 else slice(tt, S, CLS)
                                wh = whi[:, sl, kk * 512:kk * 512 + 512]
                                wl = wlo[:, sl, kk * 512:kk * 512 + 512]
                                out = ps[:, V_BANK[g][tt], :]
                                nc.tensor.matmul(out, hh[:, k, tok], wh, start=(k == 0), stop=False)
                                nc.tensor.matmul(out, hh[:, k, tok], wl, start=False, stop=False)
                                last = nc.tensor.matmul(out, hl[:, k, tok], wh, start=False, stop=(k == KT - 1))
                            if s == 3 and tt < 3:
                                last.then_inc(v_done, 1)
                        last.then_inc(slab_done, 1)

                def tile(pr, i):
                    if i >= 2:
                        pe.wait_ge(rope_read, hf * 24 + (6 * pr + i - 1))
                    elif pr == 0:
                        pe.wait_ge(v_dve, hf * 6 + 4)
                    else:
                        pe.wait_ge(qk_ready, hf * 4 + pr)
                    project(hf * 12, 12 + 6 * pr + i, i % 2)

                def scores(u):
                    pr, head, r = u // 8, u // 4 % 2, u % 4
                    e = pr % 2
                    if u % 8 == 0:
                        pe.wait_ge(qk_ready, hf * 4 + (pr + 1))
                    if u == 0:
                        pe.wait_ge(v_act, hf * 6 + 6)
                        pe.wait_ge(v_dve, hf * 6 + 6)
                        pe.wait_ge(setup, 17)
                    else:
                        pe.wait_ge(s_read, hf * UNITS + u)
                    rs = slice(r * P, r * P + P)
                    out = ps[:, SBANK, :]
                    nc.tensor.matmul(out, q0[e, "hi", head][:, rs], k0h[e][:, :], start=True, stop=False)
                    nc.tensor.matmul(out, q0[e, "lo", head][:, rs], k0h[e][:, :], start=False, stop=False)
                    nc.tensor.matmul(out, q0[e, "hi", head][:, rs], k0l[e][:, :], start=False, stop=True)
                    for g in (1, 2):
                        last = nc.tensor.matmul(ps[:, SBANK + 1, (g - 1) * P:g * P], qg[e, g, head][:, rs],
                                                kg[e, g][:, rs], start=True, stop=True)
                    last.then_inc(s_done, 1)

                def transpose(u):
                    n = hf * UNITS + u
                    if u:
                        pe.wait_ge(pt0_ready, hf * (2 * UNITS) + 2 * u)
                        pe.wait_ge(pt12_ready, n)
                    pe.wait_ge(prob_ready, n + 1)
                    for b in range(6):
                        o = PTB * 512 + b * P
                        last = nc.tensor.transpose(flat[:, o:o + P], Sb[:, u % 2, b * P:b * P + P], idn[:, :])
                    last.then_inc(pt_done, 1)

                for i in range(6):
                    tile(0, i)
                reduce_ada(hf * 4 + JOBS_START, 0)
                for u in range(UNITS + 1):
                    pr, i = u // 8 + 1, TILE_UNIT.get(u % 8)
                    if u < UNITS:
                        scores(u)
                    if u % 4 == 1 and u > 4:
                        values(hf, u // 4 - 1)
                    if i is not None and pr < HEAD_PAIRS:
                        tile(pr, i)
                    if u:
                        transpose(u - 1)
                    if u % 8 == 7 and pr < HEAD_PAIRS:
                        reduce_ada(hf * 4 + (JOBS_START + pr), pr % 2)
                values(hf, 2 * HEAD_PAIRS - 1)

            for m in range(KT):
                if m >= 2:
                    pe.wait_ge(x_upd, m - 1)
                project(WO0 // 3, m, m % 2, tiles=(hid_lo, HID_O) if m == 0 else None)

            def ffn(i, base, layer, upd):
                mean_square(i)
                for half in range(2):
                    n0 = base + half * 3 * FH
                    g0 = (HID_F1 if layer else HID_F0) + half * FH

                    def pair(q, c, t, cnt, ready):
                        pe.wait_ge(hid_lo, cnt)
                        for s in range(2):
                            project(q, c + s, 2 * (t % 3) + s, tiles=ready if s == 0 else None)

                    if half == 1:
                        pe.wait_ge(x_upd, upd + KT)
                    with pe.Fori(0, 3) as it:
                        for t in range(3):
                            pair(it * 2 + n0 // 3, n0 % 3 + 2 * t, t, it * 3 + (g0 + t - 2),
                                 (h_ready, KT * i) if half == 0 and t == 0 else None)
                            if layer == 0 and t:
                                reduce_ada(it * 2 + (JOBS_L0 + half * 6 + t - 1), t - 1)
                    for t in range(9, FH):
                        pair(0, n0 + 2 * t, t, g0 + t - 2, None)
                    for b in range(FH * KT):
                        m, k = divmod(b, FH)
                        n = n0 + 2 * FH + b // BLOCKS
                        if b % BLOCKS == 0:
                            s = slab(0, n)
                        if m == 0:
                            pe.wait_ge(hid_lo, g0 + max(k + 1, FH - 1))
                        if k == 0 and m >= 6:
                            pe.wait_ge(x_upd, upd + KT * half + m - 1)
                        last = passes(ps[:, FFO_BANK[m], :], wblk(whi, s, b % BLOCKS), wblk(wlo, s, b % BLOCKS),
                                      hidh[:, k, :], hidl[:, k, :], k == 0, k == FH - 1)
                        if k == FH - 1 and m < KT - 1:
                            last.then_inc(ffo_done, 1)
                        if b % BLOCKS == BLOCKS - 1:
                            last.then_inc(slab_done, 1)

            ffn(1, FFN0, 0, U_WO)
            mean_square(2)
            with pe.Fori(0, KT // 2) as it:
                for t in range(2):
                    pe.wait_ge(hid_lo, it * 2 + (HID_CONV + t - 1))
                    for s in range(3):
                        project(it * 2 + CONV_IN // 3, CONV_IN % 3 + 3 * t + s, 3 * t + s,
                                tiles=(h_ready, 2 * KT) if s == 0 and t == 0 else None)
            for m in range(KT):
                if m == 0:
                    pe.wait_ge(hid_lo, HID_CONV + KT - 1)
                if m >= 2:
                    pe.wait_ge(x_upd, U_F0 + m - 1)
                project(0, CONV_OUT + m, m % 2, hidh, hidl, tiles=(hid_lo, HID_CONV) if m == 0 else None)
            ffn(3, FFN1, 1, U_CO)
            mean_square(4)


def constants():
    m = np.arange(P)[:, None]
    masks = np.full((P, CLS, S + 2 * P), NEG, np.float32)
    for r in range(CLS):
        masks[:, r, :S][np.abs(CLS * m + r - np.arange(S)[None, :]) <= 64] = 0
        masks[:, r, S:S + P][np.abs(m - np.arange(P)[None, :]) <= 64] = 0
        masks[:, r, S + P:][(m - np.arange(P)[None, :]) % 4 == 0] = 0
    half = DH // 8
    inv = np.float32(500000.0) ** (-np.arange(half, dtype=np.float32) * np.float32(2.0 / (DH // 4)))
    ang = (np.arange(S, dtype=np.float32)[None, :] * inv[:, None]).astype(np.float32)
    rope = np.zeros((2, P, S), np.float32)
    rope[0] = 1
    for head in (0, DH):
        for part, sign in ((0, -1), (half, 1)):
            rope[0, head + part:head + part + half] = np.cos(ang)
            rope[1, head + part:head + part + half] = sign * np.sin(ang)
    return masks, rope, np.eye(P, dtype=np.float32)


def blocks(w):
    k, n = w.shape
    return w.reshape(k // P, P, n // P, P).transpose(2, 1, 0, 3).reshape(n // P, P, -1)


def feature_major(v):
    return np.ascontiguousarray(v.reshape(-1, P).T)


def weight_stream(qkv, wo, ffn_in, ffn_out, conv_in, conv_out):
    qkv = qkv.reshape(D, GROUPS, 3, D)
    out = []
    for half in range(2):
        for g in range(GROUPS):
            v = qkv[:, g, 2, half * 512:half * 512 + 512].reshape(4, 2, P, 512)
            out.append(v.transpose(0, 2, 1, 3).reshape(4, P, SLAB))
        for pair in range(4 * half, 4 * half + 4):
            for g in range(GROUPS):
                for which in range(2):
                    out.append(blocks(qkv[:, g, which, pair * P:pair * P + P]))
    out.append(blocks(wo))

    def ffn(w_in, w_out):
        for half in range(2):
            for t in range(half * FH, half * FH + FH):
                for o in (0, F):
                    out.append(blocks(w_in[:, o + t * P:o + t * P + P]))
            b = blocks(w_out[half * FH * P:(half + 1) * FH * P]).reshape(KT, P, FH, P)
            out.append(b.transpose(0, 2, 1, 3).reshape(FH, BLOCKS, P, P).transpose(0, 2, 1, 3).reshape(FH, P, SLAB))

    ffn(ffn_in[0], ffn_out[0])
    for m in range(KT):
        for o in (0, D, 2 * D):
            out.append(blocks(conv_in[:, o + m * P:o + m * P + P]))
    out.append(blocks(conv_out))
    ffn(ffn_in[1], ffn_out[1])
    stream = np.concatenate(out)
    assert stream.shape == (SLABS, P, SLAB)
    return stream


def kernel(x, c, attn_w_qkv, attn_w_o, conv_w_in, conv_w, conv_w_out, ada_w, ada_b, norm_mix_g, norm_ffn_g,
           ffn_w_in, ffn_w_out, final_g):
    import concourse.bacc as bacc
    from concourse.bass_utils import run_bass_kernel_spmd

    a = {k: np.asarray(v) for k, v in locals().items() if k not in ("bacc", "run_bass_kernel_spmd")}
    masks, rope, ident = constants()
    gains = np.concatenate([feature_major(g) for g in (a["norm_mix_g"][0], a["norm_ffn_g"][0], a["norm_mix_g"][1],
                                                       a["norm_ffn_g"][1], a["final_g"])], axis=1)
    arrays = {
        "xT": a["x"][0].T.reshape(KT, P, S).transpose(1, 0, 2),
        "cT": feature_major(a["c"][0]),
        "wstream": weight_stream(a["attn_w_qkv"][0], a["attn_w_o"][0], a["ffn_w_in"], a["ffn_w_out"],
                                 a["conv_w_in"][0], a["conv_w_out"][0]),
        "adaw": a["ada_w"].reshape(2, KT, P, 12, AJ).transpose(0, 3, 1, 2, 4).reshape(JOBS, KT, P, AJ),
        "adab": feature_major(a["ada_b"]),
        "gains": gains,
        "convw": a["conv_w"][0].reshape(3, KT, P).transpose(2, 1, 0).reshape(P, 3 * KT),
        "masks": masks,
        "rope": rope,
        "ident": ident,
    }
    arrays = {k: np.ascontiguousarray(v) for k, v in arrays.items()}
    nc = bacc.Bacc("TRN2", target_bir_lowering=False, num_devices=1)
    args = [nc.dram_tensor(k, v.shape, mybir.dt.from_np(v.dtype), kind="ExternalInput").ap() for k, v in arrays.items()]
    args.append(nc.dram_tensor("outT", (P, KT, S), F32, kind="ExternalOutput").ap())
    encoder(nc, *args)
    r = run_bass_kernel_spmd(nc, [arrays], core_ids=[0])
    return r.results[0]["outT"].transpose(1, 0, 2).reshape(D, S).T[None]
```

```python
from contextlib import ExitStack

import numpy as np

import concourse.bass as bass
from concourse import mybir

F32 = mybir.dt.float32
F32R = mybir.dt.float32r
ALU = mybir.AluOpType
ACT = mybir.ActivationFunctionType

P = 128
D = 1024
S = 512
KT = D // P
F = 2816
FT = F // P
FH = FT // 2
DH = 64
GROUPS = 3
CLS = 4
EPS = 1e-6
SCALE = DH ** -0.5
NEG = -1e30
WIN = DH
WSTART = (0, 16, 48, 64)
HEAD_PAIRS = 4

BLOCKS = 8
SLAB = BLOCKS * P
RING = 3
HALF_SLABS = 36
WO0 = 2 * HALF_SLABS
FFN0 = WO0 + KT
FFN_SLABS = 2 * (2 * FH + FH)
CONV_IN = FFN0 + FFN_SLABS
CONV_OUT = CONV_IN + 3 * KT
FFN1 = CONV_OUT + KT
SLABS = FFN1 + FFN_SLABS

AJ = 512
ARING = 4
JOBS_START = 4
JOBS_L0 = 12
JOBS = 24
UNITS = 4 * 2 * CLS
STEPS = 6
LEAD = 12
TILE_UNIT = {(8 * n + 7 - LEAD) // STEPS: divmod(n + 6, 6) for n in range(6 * (HEAD_PAIRS - 1))}
ALONE = 8 * (HEAD_PAIRS - 1)
LAG = 2
FFO_SLAB = tuple((FH * m + FH - 1) // BLOCKS for m in range(KT))
V_BANK = ((0, 1, 2, 3), (4, 5, 0, 1), (2, 3, 4, 5))
CHUNKS_TILE = ((0,), (1,), (2,), (3,), (), (4, 5))
CHUNKS_LAST = (6, 7)
CHUNKS_UNIT = {2: (0, 1, 2, 3), 6: (4, 5, 6, 7)}
CHUNKS_FFN = tuple(tuple(divmod(c, 8) for c in range(a, b)) for a, b in ((0, 6), (6, 11), (11, 16)))
SETUP = 1 + 2 * 2 * GROUPS
LINKS_PAIR = 24
BANKS = 6
FFO_BANK = (0, 1, 2, 3, 4, 5, 4, 5)
HID_O, HID_F0, HID_CONV, HID_F1 = 0, KT, KT + 2 * FH, 2 * KT + 2 * FH
SH1, SC1, G1, SH2, SC2, G2 = (KT * n for n in range(6))
L1 = 6 * KT


def encoder(nc, xT, cT, wstream, adaw, adab, gains, convw, masks, rope, ident, outT):
    with ExitStack() as ctx:
        at = [(nc.sbuf_base + 63) // 64 * 64]

        def sb(name, shape, dt=F32):
            t = nc.alloc_sbuf_tensor_at(name, shape, dt, offset=at[0])
            at[0] += (4 * int(np.prod(shape[1:])) + 63) // 64 * 64
            return t

        def sem(name):
            return ctx.enter_context(nc.semaphore(name))

        x = sb("x", [P, KT, S])
        hh = sb("h_hi", [P, KT, S], F32R)
        hl = sb("h_lo", [P, KT, S], F32R)
        raw = sb("w_raw", [P, RING, SLAB])
        whi = sb("w_hi", [P, RING, SLAB], F32R)
        wlo = sb("w_lo", [P, RING, SLAB], F32R)
        aring = sb("ada_ring", [P, ARING, AJ])
        acc = sb("ada_acc", [P, 2, AJ])
        modv = sb("mod", [P, 12 * KT])
        bias = sb("ada_bias", [P, 12 * KT])
        cond = sb("cond", [P, KT])
        gain = sb("gains", [P, 5 * KT])
        aff = sb("mod_gain", [P, 4 * KT])
        cw = sb("conv_w", [P, 3 * KT])
        ones = sb("ones", [P, P])
        idn = sb("ident", [P, P])
        eps = sb("eps", [P, 1])
        std = sb("rms", [P, CLS])
        rstd = sb("rstd", [P, CLS])
        region = at[0]
        cosT = sb("cos", [P, S])
        sinT = sb("sin", [P, S])
        mask = sb("mask", [P, CLS, S + 2 * P])
        V = sb("v", [P, GROUPS, CLS, S])
        q0 = {(e, b): sb(f"q0_{e}{b}", [P, S], F32R) for e in (0, 1) for b in (0, 1)}
        k0h = {(e, b): sb(f"k0_hi{e}{b}", [P, S], F32R) for e in (0, 1) for b in (0, 1)}
        k0l = {(e, b): sb(f"k0_lo{e}{b}", [P, S], F32R) for e in (0, 1) for b in (0, 1)}
        qg = {(e, g, b): sb(f"q{g}_{e}{b}", [P, S]) for e in (0, 1) for g in (1, 2) for b in (0, 1)}
        kg = {(e, g): sb(f"k{g}_{e}", [P, S]) for e in (0, 1) for g in (1, 2)}
        ropeA = sb("rope_a", [P, S])
        ropeB = sb("rope_b", [P, S])
        Sb = sb("probs", [P, 3, S + 2 * P])
        nmax = sb("neg_max", [P, 4])
        turn = sb("turn", [P, 4])
        den = sb("denom", [P, 4])
        rden = sb("denom_inv", [P, 4])
        PT0 = sb("probs_t0", [P, CLS, CLS, WIN])
        PT12 = sb("probs_t12", [P, 2, CLS, P])
        assert at[0] <= nc.sbuf_usable_end, at[0]
        at[0] = region
        hidh = sb("hid_hi", [P, FH, S], F32R)
        hidl = sb("hid_lo", [P, FH, S], F32R)
        gate = sb("gate", [P, 3, S])
        cbuf = sb("conv_c", [P, 2, S])
        cu = sb("conv_cu", [P, S + 2])
        zb = sb("conv_z", [P, S])
        sq = sb("squares", [P, KT, S])
        ssum = sb("square_sum", [P, S])
        xr = sb("x_rstd", [P, 2, S])
        assert at[0] <= nc.sbuf_usable_end, at[0]

        ps = ctx.enter_context(nc.psum_tensor("ps", [P, 8, 512], F32))
        flat = ps[:, :, :].rearrange("p b n -> p (b n)")
        MODB = 7
        SBANK, PTB, OB = 2, 4, 6
        NB = 6

        raw_in = [sem(f"raw_in{i}") for i in range(RING)]
        hi_ready = sem("hi_ready")
        lo_ready = sem("lo_ready")
        slab_done = sem("slab_done")
        ada_in = [sem(f"ada_in{i}") for i in range(ARING)]
        ada_acc = sem("ada_acc")
        ada_red = sem("ada_red")
        small_in = sem("small_in")
        tables_in = sem("tables_in")
        id_in = sem("id_in")
        x_in = sem("x_in")
        cond_ready = sem("cond_ready")
        setup = sem("setup")
        sq_ready = sem("sq_ready")
        ssum_ready = sem("ssum_ready")
        ssq_ready = sem("ssq_ready")
        std_ready = sem("std_ready")
        rstd_ready = sem("rstd_ready")
        xr_ready = sem("xr_ready")
        rb_ready = sem("rb_ready")
        part_sum = sem("part_sum")
        hhi_ready = sem("hhi_ready")
        h_ready = sem("h_ready")
        v_done = sem("v_done")
        v_act = sem("v_act")
        v_dve = sem("v_dve")
        rope_raw = sem("rope_raw")
        rope_read = sem("rope_read")
        q0_hi = sem("q0_hi")
        qk_ready = sem("qk_ready")
        s_done = sem("s_done")
        s_read = sem("s_read")
        exp_done = sem("exp_done")
        prob_ready = sem("prob_ready")
        pt_done = sem("pt_done")
        pt_ready = sem("pt_ready")
        pv_done = sem("pv_done")
        o_ready = sem("o_ready")
        x_upd = sem("x_upd")
        ffo_done = sem("ffo_done")
        gate_ready = sem("gate_ready")
        hid_hi = sem("hid_hi_ready")
        hid_lo = sem("hid_lo_ready")
        cpy_ready = sem("cpy_ready")
        y_raw = sem("y_raw")
        link_dve = sem("link_dve")
        link_cos = sem("link_cos")
        fin_ready = sem("fin_ready")
        out_done = sem("out_done")

        def wblk(t, slot, b, n=P):
            return t[:, slot, b * P:b * P + n]

        def s_bank(u):
            return SBANK if u < ALONE or u % 2 else 0

        def classes(ap):
            return ap.rearrange("p (m r) -> p r m", r=CLS)

        U_WO, U_F0, U_CO = KT, 3 * KT, 4 * KT

        block = ctx.enter_context(nc.Block())

        @block.sync
        def _(sp):
            def load_slab(q, c):
                n = 3 * q + c
                if not (isinstance(n, int) and n < RING):
                    sp.wait_ge(lo_ready, n - 2)
                sp.dma_start(raw[:, c % RING, :], wstream[n]).then_inc(raw_in[c % RING], 16)

            def load_ada(job, k):
                if not (isinstance(job, int) and job == 0 and k < ARING):
                    sp.wait_ge(ada_acc, 8 * job + k - 3)
                sp.dma_start(aring[:, k % ARING, :], adaw[job, k]).then_inc(ada_in[k % ARING], 16)

            sp.dma_start(cond[:, :], cT).then_inc(small_in, 16)
            sp.dma_start(bias[:, :], adab).then_inc(small_in, 16)
            sp.dma_start(gain[:, :], gains).then_inc(small_in, 16)
            for job in range(JOBS_START):
                for k in range(8):
                    load_ada(job, k)
                    if job < 2 and k % 2:
                        t = 4 * job + k // 2
                        sp.dma_start(x[:, t, :], xT[:, t, :]).then_inc(x_in, 16)
                    if job == JOBS_START - 1 and k == 3:
                        load_slab(0, 0)
                if job == 0:
                    sp.dma_start(idn[:, :], ident).then_inc(id_in, 16)
            for n in range(1, RING):
                load_slab(0, n)
            sp.dma_start(cw[:, :], convw).then_inc(tables_in, 16)
            sp.dma_start(cosT[:, :], rope[0]).then_inc(tables_in, 16)
            sp.dma_start(sinT[:, :], rope[1]).then_inc(tables_in, 16)
            sp.dma_start(mask[:, :, :], masks).then_inc(tables_in, 16)
            with sp.Fori(0, 2) as hf:
                with sp.Fori(0, 4) as i:
                    for c in range(3):
                        load_slab(hf * 12 + i + 1, c)
                with sp.Fori(0, 4) as pr:
                    for c in range(6):
                        load_slab(hf * 12 + pr * 2 + 5, c)
                        for k in {1: (0, 1, 2, 3), 4: (4, 5, 6, 7)}.get(c, ()):
                            load_ada(JOBS_START + hf * 4 + pr, k)
            sp.wait_ge(hid_lo, KT)
            sp.dma_start(x[:, :, :], xT).then_inc(x_in, 16)
            for m in range(KT):
                load_slab(WO0 // 3 + 1, m)
            for half in range(2):
                n0 = FFN0 + half * 3 * FH + RING
                with sp.Fori(0, 3) as i:
                    for t in range(3):
                        for jj, k in CHUNKS_FFN[t]:
                            load_ada(JOBS_L0 + half * 6 + i * 2 + jj, k)
                        for s in range(2):
                            load_slab(i * 2 + n0 // 3, n0 % 3 + 2 * t + s)
                n1 = n0 + 18
                with sp.Fori(0, 5) as i:
                    for c in range(3):
                        load_slab(i + n1 // 3, n1 % 3 + c)
            n0 = CONV_IN + RING
            trips, rest = divmod(SLABS - n0, 3)
            with sp.Fori(0, trips) as i:
                for c in range(3):
                    load_slab(i + n0 // 3, n0 % 3 + c)
            for c in range(rest):
                load_slab(trips + n0 // 3, n0 % 3 + c)
            for t in range(KT):
                sp.wait_ge(fin_ready, t + 1)
                sp.dma_start(outT[:, t, :], sq[:, t, :]).then_inc(out_done, 16)
            sp.wait_ge(out_done, 16 * KT)

        @block.gpsimd
        def _(pool):
            def low(q, c):
                n = 3 * q + c
                pool.wait_ge(hi_ready, n + 1)
                s = c % RING
                nc.gpsimd.tensor_tensor(wlo[:, s, :], raw[:, s, :], whi[:, s, :].bitcast(F32),
                                        ALU.subtract).then_inc(lo_ready, 1)

            for t in range(1, KT - 1):
                pool.wait_ge(sq_ready, t + 1)
                if t > 1:
                    pool.wait_ge(part_sum, t - 1)
                ins = nc.gpsimd.tensor_tensor(ssum[:, :], sq[:, 0, :] if t == 1 else ssum[:, :], sq[:, t, :], ALU.add)
                ins.then_inc(part_sum if t < KT - 2 else ssum_ready, 1)
            trips, rest = divmod(SLABS, 3)
            with pool.Fori(0, trips) as i:
                for c in range(3):
                    low(i, c)
            for c in range(rest):
                low(trips, c)

        @block.scalar
        def _(act):
            def high(q, c):
                n = 3 * q + c
                if isinstance(n, int):
                    if n >= SLABS:
                        return
                    if n >= RING:
                        act.wait_ge(slab_done, n - 2)
                else:
                    act.wait_ge(slab_done, n - 2)
                act.wait_ge(raw_in[c % RING], (q + c // RING) * 16 + 16)
                nc.scalar.copy(whi[:, c % RING, :], raw[:, c % RING, :]).then_inc(hi_ready, 1)

            def square(i, t, upd):
                if upd is None:
                    act.wait_ge(x_in, 16 * KT)
                else:
                    act.wait_ge(x_upd, upd + t + 1)
                nc.scalar.activation(sq[:, t, :], x[:, t, :], ACT.Square).then_inc(sq_ready, 1)

            def root(i):
                act.wait_ge(ssq_ready, i + 1)
                nc.scalar.activation(std[:, :], ps[:, NB, 0:CLS], ACT.Sqrt, bias=eps[:, 0:1],
                                     scale=1.0 / D).then_inc(std_ready, 1)

            def norm_out(i, vec, tiles=range(KT)):
                for t in tiles:
                    act.wait_ge(xr_ready, i * KT + t + 1)
                    nc.scalar.activation(hh[:, t, :], xr[:, t % 2, :], ACT.Identity,
                                         bias=modv[:, vec + t:vec + t + 1]).then_inc(hhi_ready, 1)

            act.wait_ge(small_in, 48)
            nc.scalar.activation(cond[:, :], cond[:, :], ACT.Silu).then_inc(cond_ready, 1)
            for t in range(KT):
                square(0, t, None)
            root(0)
            high(0, 0)
            norm_out(0, SH1, range(4))
            high(0, 1)
            norm_out(0, SH1, range(4, KT))
            high(0, 2)
            with act.Fori(0, 2) as hf:
                for g in range(GROUPS):
                    for s in range(4):
                        high(hf * 12, 4 * g + s + RING)
                    for tt in (0, 1):
                        act.wait_ge(v_done, hf * 9 + 3 * g + tt + 1)
                        nc.scalar.copy(V[:, g, tt, :], ps[:, V_BANK[g][tt], :]).then_inc(v_act, 1)

                def tile_parts(pr, i):
                    e = pr % 2
                    if i < 2:
                        act.wait_ge(rope_raw, hf * 8 + 2 * pr + i + 1)
                    if i == 0:
                        for b in (0, 1):
                            r = slice(DH * b, DH * b + DH)
                            nc.scalar.copy(q0[e, b][r, :].rearrange("p (r m) -> p r m", r=CLS),
                                           classes(ropeA[r, :])).then_inc(q0_hi, 1)
                    if i == 1:
                        for other in (0, 1):
                            for b in (0, 1):
                                r, to = slice(DH * b, DH * b + DH), DH * (b ^ other)
                                nc.scalar.copy(k0h[e, b][to:to + DH, :], ropeA[r, :]).then_inc(q0_hi, 1)

                def probs(u):
                    n = hf * UNITS + u
                    act.wait_ge(s_read, n + 1)
                    nc.scalar.activation(Sb[:, u % 3, :], Sb[:, u % 3, :], ACT.Exp,
                                         bias=nmax[:, u % 4:u % 4 + 1], scale=-1.0,
                                         accum_out=den[:, u % 4:u % 4 + 1]).then_inc(exp_done, 1)

                def take_t(u):
                    if u % 4 == 0 and u:
                        act.wait_ge(pv_done, hf * 8 + u // 4)
                    act.wait_ge(pt_done, hf * UNITS + u + 1)
                    for h2 in (0, 1):
                        o = PTB * 512 + 304 * h2
                        src = flat[:, o:o + 288].rearrange("p (t n) -> p t n", t=2)[:, :, 0:WIN]
                        nc.scalar.copy(PT0[:, 2 * h2:2 * h2 + 2, u % 4, :], src)
                    nc.scalar.copy(PT12[:, :, u % 4, :],
                                   ps[:, PTB + 1, 0:256].rearrange("p (g n) -> p g n", g=2)).then_inc(pt_ready, 1)

                def take_o(pr):
                    act.wait_ge(pv_done, hf * 8 + (2 * pr + 2))
                    nc.scalar.copy(x[:, bass.ds(hf * 4 + pr, 1), :].rearrange("p a (m r) -> p (a r) m", r=CLS),
                                   ps[:, OB, :].rearrange("p (r m) -> p r m", r=CLS)).then_inc(o_ready, 1)

                for i in range(6):
                    high(hf * 12, 12 + i + RING)
                    tile_parts(0, i)
                for u in range(-1, UNITS + LAG):
                    if u >= ALONE:
                        take_t(u - LAG)
                    if 0 <= u < UNITS:
                        probs(u)
                    if u in TILE_UNIT:
                        pr, i = TILE_UNIT[u]
                        high(hf * 12, 12 + 6 * pr + i + RING)
                        tile_parts(pr, i)
                    if LAG <= u < ALONE:
                        take_t(u - LAG)
                    if u % 8 == LAG and u > 8:
                        take_o(u // 8 - 1)
                take_o(HEAD_PAIRS - 1)
            for t in range(KT):
                act.wait_ge(o_ready, t + 1)
                nc.scalar.copy(hh[:, t, :], x[:, t, :]).then_inc(hid_hi, 1)
            for m in range(KT):
                high(WO0 // 3, m + RING)
                square(1, m, 0)

            def ffn(i, base, upd):
                root(i)
                norm_out(i, SH2 if i == 1 else L1 + SH2)
                for half in range(2):
                    n0 = base + half * 3 * FH

                    def gated(slabs, t):
                        act.wait_ge(slab_done, slabs)
                        nc.scalar.activation(gate[:, t % 3, :], ps[:, 2 * (t % 3), :],
                                             ACT.Silu).then_inc(gate_ready, 1)

                    with act.Fori(0, 3) as it:
                        for t in range(3):
                            gated(it * 6 + (n0 + 2 * t + 1), t)
                            for s in range(2):
                                high(it * 2 + n0 // 3, n0 % 3 + 2 * t + s + RING)
                    for t in range(9, FH):
                        gated(n0 + 2 * t + 1, t)
                        for s in range(2):
                            high(0, n0 + 2 * t + s + RING)
                    for s in range(FH):
                        high(0, n0 + 2 * FH + s + RING)
                        if half and s in FFO_SLAB:
                            square(i + 1, FFO_SLAB.index(s), upd + KT)

            ffn(1, FFN0, U_WO)
            root(2)
            norm_out(2, L1 + SH1)
            with act.Fori(0, KT // 2) as it:
                for t in range(2):
                    for s in range(3):
                        high(it * 2 + CONV_IN // 3, CONV_IN % 3 + 3 * t + s + RING)
                    act.wait_ge(slab_done, it * 6 + (CONV_IN + 3 * t + 2))
                    nc.scalar.copy(cbuf[:, t, :], ps[:, 3 * t + 1, :]).then_inc(cpy_ready, 1)
            for m in range(KT):
                high(0, CONV_OUT + m + RING)
                square(3, m, U_F0)
            ffn(3, FFN1, U_CO)
            root(4)

        @block.vector
        def _(dve):
            step = {"base": 0, "n": 0}

            def link(ins):
                step["n"] += 1
                ins.then_inc(link_dve, 1)
                dve.wait_ge(link_dve, step["base"] + step["n"])

            def enter(reg, per):
                step["saved"] = step["base"] + step["n"]
                step["base"], step["n"], step["per"] = reg * per + step["saved"], 0, per

            def leave(trips):
                assert step["n"] == step["per"], step
                step["base"], step["n"] = step["saved"] + trips * step["per"], 0

            def ada_chunk(job, k, par):
                dve.wait_ge(ada_in[k % ARING], job * 32 + 16 * (k // ARING) + 16)
                src = aring[:, k % ARING, :]
                if k == 0:
                    if isinstance(job, int) and 2 <= job < JOBS_START:
                        dve.wait_ge(ada_red, job - 1)
                    nc.vector.tensor_scalar(acc[:, par, :], src, cond[:, 0:1], None, ALU.mult).then_inc(ada_acc, 1)
                else:
                    dve.wait_ge(ada_acc, job * 8 + k)
                    nc.vector.scalar_tensor_tensor(out=acc[:, par, :], in0=src, scalar=cond[:, k:k + 1],
                                                   in1=acc[:, par, :],
                                                   op0=ALU.mult, op1=ALU.add).then_inc(ada_acc, 1)

            def mod_add(job, jobs):
                dve.wait_ge(ada_red, job + jobs)
                c = bass.ds(job * 4, 4 * jobs)
                link(nc.vector.tensor_tensor(modv[:, c], ps[:, MODB, c], bias[:, c], ALU.add))

            def add_square(i, t):
                if 0 < t < KT - 1:
                    dve.wait_ge(sq_ready, i * KT + t + 1)
                if t == 1:
                    link(nc.vector.tensor_tensor(ssum[:, :], sq[:, 0, :], sq[:, 1, :], ALU.add))
                elif 1 < t < KT - 2:
                    link(nc.vector.tensor_tensor(ssum[:, :], ssum[:, :], sq[:, t, :], ALU.add))
                elif t == KT - 2:
                    nc.vector.tensor_tensor(ssum[:, :], ssum[:, :], sq[:, t, :], ALU.add).then_inc(ssum_ready, 1)

            def inverse(i):
                dve.wait_ge(std_ready, i + 1)
                nc.vector.reciprocal(rstd[:, :], std[:, :]).then_inc(rstd_ready, 1)

            def norm(i, vec):
                if vec is not None:
                    a = slice(KT * i, KT * i + KT)
                    sc = slice(vec, vec + KT)
                    link(nc.vector.scalar_tensor_tensor(out=aff[:, a], in0=modv[:, sc], scalar=1.0,
                                                        in1=gain[:, KT * i:KT * i + KT],
                                                        op0=ALU.add, op1=ALU.mult))
                if i:
                    inverse(i)
                dve.wait_ge(rb_ready, i + 1)
                for t in range(KT):
                    if vec is None:
                        nc.vector.scalar_tensor_tensor(out=sq[:, t, :], in0=x[:, t, :],
                                                       scalar=gain[:, KT * i + t:KT * i + t + 1],
                                                       in1=ps[:, NB, :], op0=ALU.mult,
                                                       op1=ALU.mult).then_inc(fin_ready, 1)
                        continue
                    if i * KT + t >= 2:
                        dve.wait_ge(h_ready, i * KT + t - 1)
                    nc.vector.scalar_tensor_tensor(out=xr[:, t % 2, :], in0=x[:, t, :],
                                                   scalar=aff[:, KT * i + t:KT * i + t + 1], in1=ps[:, NB, :],
                                                   op0=ALU.mult, op1=ALU.mult).then_inc(xr_ready, 1)
                    if t:
                        low_h(i, t - 1, vec - KT)
                if vec is not None:
                    low_h(i, KT - 1, vec - KT)

            def low_h(i, t, vec):
                dve.wait_ge(hhi_ready, i * KT + t + 1)
                nc.vector.scalar_tensor_tensor(out=hl[:, t, :], in0=xr[:, t % 2, :],
                                               scalar=modv[:, vec + t:vec + t + 1],
                                               in1=hh[:, t, :].bitcast(F32), op0=ALU.add,
                                               op1=ALU.subtract).then_inc(h_ready, 1)

            nc.vector.memset(eps[:, :], EPS)
            nc.vector.memset(ones[:, :], 1.0).then_inc(setup, 1)
            dve.wait_ge(cond_ready, 1)
            for job in range(JOBS_START):
                for k in range(8):
                    ada_chunk(job, k, job % 2)
                    if job == JOBS_START - 1 and k == 5:
                        inverse(0)
            mod_add(0, JOBS_START)
            norm(0, SC1)
            dve.wait_ge(h_ready, KT)
            for e in (0, 1):
                for b in (0, 1):
                    r = slice(DH * (1 - b), DH * (1 - b) + DH)
                    nc.vector.memset(k0l[e, b][r, :].bitcast(F32), 0.0).then_inc(setup, 1)
                    for g in (1, 2):
                        nc.vector.memset(qg[e, g, b][r, :], 0.0).then_inc(setup, 1)

            swap = [(j + 8) % 16 if j < 16 else j for j in range(32)]
            with dve.Fori(0, 2) as hf:
                enter(hf, HEAD_PAIRS * LINKS_PAIR)
                for g in range(GROUPS):
                    for tt in (2, 3):
                        if tt == 2:
                            dve.wait_ge(v_done, hf * 9 + 3 * g + 3)
                        else:
                            dve.wait_ge(slab_done, hf * HALF_SLABS + 4 * g + 4)
                        nc.vector.tensor_copy(V[:, g, tt, :], ps[:, V_BANK[g][tt], :]).then_inc(v_dve, 1)

                def chunks(pr, some):
                    for k in some:
                        ada_chunk(hf * 4 + (JOBS_START + pr), k, pr % 2)

                def rotate(pr, i):
                    g, is_k, e = i // 2, i % 2, pr % 2
                    dve.wait_ge(slab_done, hf * HALF_SLABS + (12 + 6 * pr + i + 1))
                    if i == 1 or i == 2:
                        dve.wait_ge(q0_hi, hf * 24 + (6 * pr + (2 if i == 1 else 6)))
                    if pr and i == 0:
                        dve.wait_ge(qk_ready, hf * 4 + pr)
                    if pr == 0 and i == 0:
                        dve.wait_ge(tables_in, 64)
                    nc.vector.tensor_tensor(ropeA[:, :], ps[:, i % 2, :], cosT[:, :],
                                            ALU.mult).then_inc(link_cos, 1)
                    nc.vector.stream_shuffle(ropeB[:, :], ps[:, i % 2, :], swap).then_inc(rope_read, 1)
                    dve.wait_ge(rope_read, hf * 24 + (6 * pr + i + 1))
                    link(nc.vector.tensor_tensor(ropeB[:, :], ropeB[:, :], sinT[:, :], ALU.mult))
                    dve.wait_ge(link_cos, hf * 24 + (6 * pr + i + 1))
                    if g == 0:
                        nc.vector.tensor_tensor(ropeA[:, :], ropeA[:, :], ropeB[:, :],
                                                ALU.add).then_inc(rope_raw, 1)
                        for b in (0, 1):
                            r, o = slice(DH * b, DH * b + DH), slice(DH * (1 - b), DH * (1 - b) + DH)
                            dve.wait_ge(q0_hi, hf * 24 + (6 * pr + 2 * is_k + b + 1))
                            if is_k:
                                link(nc.vector.tensor_tensor(k0l[e, b][r, :], ropeA[r, :],
                                                             k0h[e, b][r, :].bitcast(F32), ALU.subtract))
                            else:
                                link(nc.vector.tensor_tensor(
                                    q0[e, b][o, :].rearrange("p (r m) -> p r m", r=CLS), classes(ropeA[r, :]),
                                    q0[e, b][r, :].bitcast(F32).rearrange("p (r m) -> p r m", r=CLS),
                                    ALU.subtract))
                    elif is_k:
                        ins = nc.vector.tensor_tensor(kg[e, g][:, :].rearrange("p (r m) -> p r m", r=CLS),
                                                      classes(ropeA[:, :]), classes(ropeB[:, :]), ALU.add)
                        if g == 2:
                            ins.then_inc(qk_ready, 1)
                        else:
                            link(ins)
                    else:
                        for b in (0, 1):
                            r = slice(DH * b, DH * b + DH)
                            link(nc.vector.tensor_tensor(
                                qg[e, g, b][r, :].rearrange("p (r m) -> p r m", r=CLS),
                                classes(ropeA[r, :]), classes(ropeB[r, :]), ALU.add))

                def masked(u):
                    dve.wait_ge(s_done, hf * UNITS + (u + 1))
                    nc.vector.memset(turn[:, u % 4:u % 4 + 1], 0.0)
                    nc.vector.tensor_tensor_reduce(
                        Sb[:, u % 3, :], flat[:, s_bank(u) * 512:s_bank(u) * 512 + 768], mask[:, u % 4, :],
                        -SCALE, 3e38, ALU.add, ALU.min, nmax[:, u % 4:u % 4 + 1]).then_inc(s_read, 1)

                def normalise(u):
                    dve.wait_ge(exp_done, hf * UNITS + (u + 1))
                    link(nc.vector.reciprocal(rden[:, u % 4:u % 4 + 1], den[:, u % 4:u % 4 + 1]))
                    nc.vector.tensor_scalar(Sb[:, u % 3, :], Sb[:, u % 3, :], rden[:, u % 4:u % 4 + 1],
                                            None, ALU.mult).then_inc(prob_ready, 1)

                for i in range(6):
                    rotate(0, i)
                    chunks(0, CHUNKS_TILE[i])
                for u in range(-1, UNITS + LAG):
                    pr = u // 8 + 1
                    if 0 <= u < UNITS:
                        masked(u)
                    if 0 < u <= UNITS:
                        normalise(u - 1)
                    if u >= 0 and pr < HEAD_PAIRS:
                        chunks(pr, CHUNKS_UNIT.get(u % 8, ()))
                    if u in TILE_UNIT:
                        rotate(*TILE_UNIT[u])
                    if u == -1:
                        chunks(0, CHUNKS_LAST)
                    if u == 1:
                        mod_add(hf * 4 + JOBS_START, 1)
                    if u >= 0 and u % 8 == 7 and pr < HEAD_PAIRS:
                        mod_add(hf * 4 + (JOBS_START + pr), 1)
                leave(2)

            for t in range(KT):
                dve.wait_ge(hid_hi, t + 1)
                nc.vector.tensor_tensor(hl[:, t, :], x[:, t, :], hh[:, t, :].bitcast(F32),
                                        ALU.subtract).then_inc(hid_lo, 1)

            def residual(src, gvec, m):
                nc.vector.scalar_tensor_tensor(out=x[:, m, :], in0=src, scalar=modv[:, gvec + m:gvec + m + 1],
                                               in1=x[:, m, :], op0=ALU.mult, op1=ALU.add).then_inc(x_upd, 1)

            for m in range(KT):
                dve.wait_ge(slab_done, WO0 + m + 1)
                if m == 0:
                    dve.wait_ge(x_in, 16 * (KT + 1))
                residual(ps[:, m % BANKS, :], G1, m)
                if m:
                    add_square(1, m - 1)

            def ffn(i, base, layer, upd):
                norm(i, layer * L1 + SC2)
                for half in range(2):
                    n0 = base + half * 3 * FH
                    g0 = (HID_F1 if layer else HID_F0) + half * FH
                    gates = (2 * layer + half) * FH

                    def hidden(slabs, cnt, t, dst):
                        dve.wait_ge(slab_done, slabs)
                        dve.wait_ge(gate_ready, dst + (gates + 1))
                        gt = gate[:, t % 3, :]
                        link(nc.vector.tensor_tensor(gt, gt, ps[:, 2 * (t % 3) + 1, :], ALU.mult))
                        hi = hidh[:, bass.ds(dst, 1), :].rearrange("p a n -> p (a n)")
                        lo = hidl[:, bass.ds(dst, 1), :].rearrange("p a n -> p (a n)")
                        nc.vector.tensor_copy(hi, gt).then_inc(hid_hi, 1)
                        dve.wait_ge(hid_hi, cnt + 1)
                        nc.vector.tensor_tensor(lo, gt, hi.bitcast(F32), ALU.subtract).then_inc(hid_lo, 1)

                    with dve.Fori(0, 3) as it:
                        enter(it, 3 + (layer == 0))
                        job = it * 2 + (JOBS_L0 + half * 6)
                        for t in range(3):
                            if layer == 0:
                                for jj, k in CHUNKS_FFN[t]:
                                    ada_chunk(job + jj, k, jj)
                            hidden(it * 6 + (n0 + 2 * t + 2), it * 3 + (g0 + t), t, it * 3 + t)
                        if layer == 0:
                            mod_add(job, 2)
                        leave(3)
                    for t in range(9, FH):
                        hidden(n0 + 2 * t + 2, g0 + t, t, t)
                    for m in range(KT):
                        if m < KT - 1:
                            dve.wait_ge(ffo_done, (2 * layer + half) * (KT - 1) + m + 1)
                        else:
                            dve.wait_ge(slab_done, n0 + 3 * FH)
                        if half:
                            dve.wait_ge(x_upd, upd + m + 1)
                        residual(ps[:, FFO_BANK[m], :], layer * L1 + G2, m)
                        if half and m:
                            add_square(i + 1, m - 1)

            ffn(1, FFN0, 0, U_WO)
            norm(2, L1 + SC1)
            link(nc.vector.memset(cu[:, :], 0.0))
            with dve.Fori(0, KT // 2) as it:
                enter(it, 2 * 4)
                for t in range(2):
                    m = it * 2 + t
                    dve.wait_ge(slab_done, it * 6 + (CONV_IN + 3 * t + 3))
                    dve.wait_ge(cpy_ready, m + 1)
                    link(nc.vector.tensor_tensor(cu[:, 1:S + 1], cbuf[:, t, :], ps[:, 3 * t + 2, :], ALU.mult))
                    link(nc.vector.tensor_scalar(zb[:, :], cu[:, 0:S], cw[:, bass.ds(m * 3, 1)], None, ALU.mult))
                    for w in (1, 2):
                        link(nc.vector.scalar_tensor_tensor(out=zb[:, :], in0=cu[:, w:S + w],
                                                            scalar=cw[:, bass.ds(m * 3 + w, 1)], in1=zb[:, :],
                                                            op0=ALU.mult, op1=ALU.add))
                    nc.vector.tensor_tensor(zb[:, :], zb[:, :], ps[:, 3 * t, :], ALU.mult).then_inc(y_raw, 1)
                    dve.wait_ge(y_raw, m + 1)
                    hi = hidh[:, bass.ds(m, 1), :].rearrange("p a n -> p (a n)")
                    lo = hidl[:, bass.ds(m, 1), :].rearrange("p a n -> p (a n)")
                    nc.vector.tensor_copy(hi, zb[:, :]).then_inc(hid_hi, 1)
                    dve.wait_ge(hid_hi, m + (HID_CONV + 1))
                    nc.vector.tensor_tensor(lo, zb[:, :], hi.bitcast(F32), ALU.subtract).then_inc(hid_lo, 1)
                leave(KT // 2)
            for m in range(KT):
                dve.wait_ge(slab_done, CONV_OUT + m + 1)
                residual(ps[:, m % BANKS, :], L1 + G1, m)
                if m:
                    add_square(3, m - 1)
            ffn(3, FFN1, 1, U_CO)
            norm(4, None)

        @block.tensor
        def _(pe):
            def passes(out, w_hi, w_lo, a_hi, a_lo, first, last):
                nc.tensor.matmul(out, w_hi, a_hi, start=first, stop=False)
                nc.tensor.matmul(out, w_hi, a_lo, start=False, stop=False)
                return nc.tensor.matmul(out, w_lo, a_hi, start=False, stop=last)

            def slab(q, c):
                pe.wait_ge(lo_ready, 3 * q + c + 1)
                return c % RING

            def project(q, c, bank, ah=hh, al=hl):
                s = slab(q, c)
                for k in range(KT):
                    last = passes(ps[:, bank, :], wblk(whi, s, k), wblk(wlo, s, k), ah[:, k, :], al[:, k, :],
                                  k == 0, k == KT - 1)
                last.then_inc(slab_done, 1)

            def project_two(q, c, ah, al, made, before):
                for s in range(2):
                    slab(q, c + s)
                for k in range(KT):
                    pe.wait_ge(made, before + k + 1)
                    for s in range(2):
                        i = (c + s) % RING
                        last = passes(ps[:, s, :], wblk(whi, i, k), wblk(wlo, i, k), ah[:, k, :], al[:, k, :],
                                      k == 0, k == KT - 1)
                        if k == KT - 1:
                            last.then_inc(slab_done, 1)

            def reduce_ada(job, par):
                pe.wait_ge(ada_acc, job * 8 + 8)
                for c in range(AJ // P):
                    last = nc.tensor.matmul(ps[:, MODB, bass.ds(job * 4 + c, 1)], acc[:, par, c * P:c * P + P],
                                            ones[:, 0:1], start=True, stop=True)
                last.then_inc(ada_red, 1)

            def mean_square(i):
                pe.wait_ge(ssum_ready, i + 1)
                for t in range(CLS):
                    nc.tensor.matmul(ps[:, NB, t:t + 1], ssum[:, t * P:t * P + P], ones[:, 0:1],
                                     start=(t == 0), stop=False)
                pe.wait_ge(sq_ready, KT * (i + 1))
                for t in range(CLS):
                    last = nc.tensor.matmul(ps[:, NB, t:t + 1], sq[:, KT - 1, t * P:t * P + P], ones[:, 0:1],
                                            start=False, stop=(t == CLS - 1))
                last.then_inc(ssq_ready, 1)
                pe.wait_ge(rstd_ready, i + 1)
                for t in range(CLS):
                    last = nc.tensor.matmul(ps[:, NB, t * P:t * P + P], rstd[:, t:t + 1].to_broadcast([P, P]),
                                            idn[:, :],
                                            start=(t == 0), stop=(t == CLS - 1))
                last.then_inc(rb_ready, 1)

            def values(hf, n):
                pr, head = divmod(n, 2)
                units = hf * UNITS + (4 * n + 4)
                pe.wait_ge(pt_ready, units)
                if head == 0 and pr:
                    pe.wait_ge(o_ready, hf * 4 + pr)
                rows = slice(DH * head, DH * head + DH)
                cols = slice(pr * P + DH * head, pr * P + DH * head + DH)
                for g in (1, 2):
                    for r in range(CLS):
                        nc.tensor.matmul(ps[rows, OB, r * P:r * P + P], V[:, g, r, cols], PT12[:, g - 1, r, :],
                                         start=(g == 1 and r == 0), stop=False)
                out = ps[rows, OB, :].rearrange("p (r m) -> p r m", r=CLS)
                for t in range(CLS):
                    last = nc.tensor.matmul(out[:, :, WSTART[t]:WSTART[t] + WIN], V[:, 0, t, cols], PT0[:, t, :, :],
                                            start=False, stop=(t == CLS - 1))
                last.then_inc(pv_done, 1)

            pe.wait_ge(setup, 1)
            for job in range(JOBS_START):
                if job == JOBS_START - 1:
                    pe.wait_ge(id_in, 16)
                    mean_square(0)
                reduce_ada(job, job % 2)
            with pe.Fori(0, 2) as hf:
                for g in range(GROUPS):
                    for s in range(4):
                        sl = slab(hf * 12, 4 * g + s)
                        for tt in range(CLS):
                            if s == 0 and (g == 2 or (g == 1 and tt > 1)):
                                copied, n = (v_act, 2 * g + tt - 3) if tt > 1 else (v_dve, tt + 1)
                                pe.wait_ge(copied, hf * 6 + n)
                            for kk in range(2):
                                k = 2 * s + kk
                                if g == 0 and tt == 0:
                                    pe.wait_ge(h_ready, k + 1)
                                tok = slice(tt * P, tt * P + P) if g == 0 else slice(tt, S, CLS)
                                wh = whi[:, sl, kk * 512:kk * 512 + 512]
                                wl = wlo[:, sl, kk * 512:kk * 512 + 512]
                                out = ps[:, V_BANK[g][tt], :]
                                nc.tensor.matmul(out, hh[:, k, tok], wh, start=(k == 0), stop=False)
                                nc.tensor.matmul(out, hh[:, k, tok], wl, start=False, stop=False)
                                last = nc.tensor.matmul(out, hl[:, k, tok], wh, start=False, stop=(k == KT - 1))
                            if s == 3 and tt < 3:
                                last.then_inc(v_done, 1)
                        last.then_inc(slab_done, 1)

                def steps(first, last):
                    for step in range(first, last):
                        tile, k = divmod(step, KT)
                        c, bank = 12 + tile, tile % 2
                        if k == 0:
                            if tile >= 2:
                                pe.wait_ge(rope_read, hf * 24 + (tile - 1))
                            else:
                                pe.wait_ge(v_dve, hf * 6 + 4)
                            slab(hf * 12, c)
                        ins = passes(ps[:, bank, :], wblk(whi, c % RING, k), wblk(wlo, c % RING, k), hh[:, k, :],
                                     hl[:, k, :], k == 0, k == KT - 1)
                        if k == KT - 1:
                            ins.then_inc(slab_done, 1)

                def scores(u):
                    pr, head, r = u // 8, u // 4 % 2, u % 4
                    e = pr % 2
                    if u % 8 == 0:
                        pe.wait_ge(qk_ready, hf * 4 + (pr + 1))
                    if u == 0:
                        pe.wait_ge(v_act, hf * 6 + 6)
                        pe.wait_ge(v_dve, hf * 6 + 6)
                        pe.wait_ge(setup, SETUP)
                    elif u < ALONE:
                        pe.wait_ge(s_read, hf * UNITS + u)
                    elif u > ALONE:
                        pe.wait_ge(s_read, hf * UNITS + u - 1)
                    rs = slice(r * P, r * P + P)
                    bank = s_bank(u)
                    out = ps[:, bank, :]
                    nc.tensor.matmul(out, q0[e, head][:, rs], k0h[e, head][:, :], start=True, stop=False)
                    nc.tensor.matmul(out, q0[e, head][:, rs], k0l[e, head][:, :], start=False, stop=True)
                    for g in (1, 2):
                        last = nc.tensor.matmul(ps[:, bank + 1, (g - 1) * P:g * P], qg[e, g, head][:, rs],
                                                kg[e, g][:, rs], start=True, stop=True)
                    last.then_inc(s_done, 1)

                def transpose(u):
                    n = hf * UNITS + u
                    if u:
                        pe.wait_ge(pt_ready, n)
                    pe.wait_ge(prob_ready, n + 1)
                    for b in range(6):
                        o = PTB * 512 + b * P
                        last = nc.tensor.transpose(flat[:, o:o + P], Sb[:, u % 3, b * P:b * P + P], idn[:, :])
                    last.then_inc(pt_done, 1)

                pair_steps = 6 * KT
                steps(0, pair_steps)
                steps(pair_steps, pair_steps + LEAD)
                for u in range(UNITS + LAG):
                    pr = u // 8 + 1
                    if u < UNITS:
                        scores(u)
                    if u == 1:
                        reduce_ada(hf * 4 + JOBS_START, 0)
                    if u % 8 == 7 and pr < HEAD_PAIRS:
                        reduce_ada(hf * 4 + (JOBS_START + pr), pr % 2)
                    step = pair_steps + LEAD + STEPS * u
                    steps(step, min(step + STEPS, HEAD_PAIRS * pair_steps))
                    if u % 4 == LAG and u > 4:
                        values(hf, u // 4 - 1)
                    if u >= LAG:
                        transpose(u - LAG)
                values(hf, 2 * HEAD_PAIRS - 1)

            project_two(WO0 // 3, 0, hh, hl, hid_lo, HID_O)
            for m in range(2, KT):
                if m >= BANKS:
                    pe.wait_ge(x_upd, m - BANKS + 1)
                project(WO0 // 3, m, m % BANKS)

            def ffn(i, base, layer, upd):
                mean_square(i)
                for half in range(2):
                    n0 = base + half * 3 * FH
                    g0 = (HID_F1 if layer else HID_F0) + half * FH

                    def pair(q, c, t, cnt, ready):
                        pe.wait_ge(hid_lo, cnt)
                        if ready is not None:
                            project_two(q, c, hh, hl, h_ready, ready)
                            return
                        for s in range(2):
                            project(q, c + s, 2 * (t % 3) + s)

                    with pe.Fori(0, 3) as it:
                        for t in range(3):
                            if half:
                                pe.wait_ge(x_upd, upd + (2, 4, KT)[t])
                            pair(it * 2 + n0 // 3, n0 % 3 + 2 * t, t, it * 3 + (g0 + t - 2),
                                 KT * i if half == 0 and t == 0 else None)
                            if layer == 0 and t:
                                reduce_ada(it * 2 + (JOBS_L0 + half * 6 + t - 1), t - 1)
                    for t in range(9, FH):
                        pair(0, n0 + 2 * t, t, g0 + t - 2, None)
                    for b in range(FH * KT):
                        m, k = divmod(b, FH)
                        n = n0 + 2 * FH + b // BLOCKS
                        if b % BLOCKS == 0:
                            s = slab(0, n)
                        if m == 0:
                            pe.wait_ge(hid_lo, g0 + max(k + 1, FH - 1))
                        if k == 0 and m >= 6:
                            pe.wait_ge(x_upd, upd + KT * half + m - 1)
                        last = passes(ps[:, FFO_BANK[m], :], wblk(whi, s, b % BLOCKS), wblk(wlo, s, b % BLOCKS),
                                      hidh[:, k, :], hidl[:, k, :], k == 0, k == FH - 1)
                        if k == FH - 1 and m < KT - 1:
                            last.then_inc(ffo_done, 1)
                        if b % BLOCKS == BLOCKS - 1:
                            last.then_inc(slab_done, 1)

            ffn(1, FFN0, 0, U_WO)
            mean_square(2)
            with pe.Fori(0, KT // 2) as it:
                for t in range(2):
                    pe.wait_ge(hid_lo, it * 2 + (HID_CONV + t - 1))
                    q, c = it * 2 + CONV_IN // 3, CONV_IN % 3 + 3 * t
                    if t == 0:
                        project_two(q, c, hh, hl, h_ready, 2 * KT)
                    for s in range(0 if t else 2, 3):
                        project(q, c + s, 3 * t + s)
            pe.wait_ge(hid_lo, HID_CONV + KT - 1)
            project_two(0, CONV_OUT, hidh, hidl, hid_lo, HID_CONV)
            for m in range(2, KT):
                if m >= BANKS:
                    pe.wait_ge(x_upd, U_F0 + m - BANKS + 1)
                project(0, CONV_OUT + m, m % BANKS, hidh, hidl)
            ffn(3, FFN1, 1, U_CO)
            mean_square(4)


def constants():
    m = np.arange(P)[:, None]
    masks = np.full((P, CLS, S + 2 * P), NEG, np.float32)
    for r in range(CLS):
        masks[:, r, :S][np.abs(CLS * m + r - np.arange(S)[None, :]) <= 64] = 0
        masks[:, r, S:S + P][np.abs(m - np.arange(P)[None, :]) <= 64] = 0
        masks[:, r, S + P:][(m - np.arange(P)[None, :]) % 4 == 0] = 0
    half = DH // 8
    inv = np.float32(500000.0) ** (-np.arange(half, dtype=np.float32) * np.float32(2.0 / (DH // 4)))
    ang = (np.arange(S, dtype=np.float32)[None, :] * inv[:, None]).astype(np.float32)
    rope = np.zeros((2, P, S), np.float32)
    rope[0] = 1
    for head in (0, DH):
        for part, sign in ((0, -1), (half, 1)):
            rope[0, head + part:head + part + half] = np.cos(ang)
            rope[1, head + part:head + part + half] = sign * np.sin(ang)
    return masks, rope, np.eye(P, dtype=np.float32)


def blocks(w):
    k, n = w.shape
    return w.reshape(k // P, P, n // P, P).transpose(2, 1, 0, 3).reshape(n // P, P, -1)


def feature_major(v):
    return np.ascontiguousarray(v.reshape(-1, P).T)


def weight_stream(qkv, wo, ffn_in, ffn_out, conv_in, conv_out):
    qkv = qkv.reshape(D, GROUPS, 3, D)
    out = []
    for half in range(2):
        for g in range(GROUPS):
            v = qkv[:, g, 2, half * 512:half * 512 + 512].reshape(4, 2, P, 512)
            out.append(v.transpose(0, 2, 1, 3).reshape(4, P, SLAB))
        for pair in range(4 * half, 4 * half + 4):
            for g in range(GROUPS):
                for which in range(2):
                    out.append(blocks(qkv[:, g, which, pair * P:pair * P + P]))
    out.append(blocks(wo))

    def ffn(w_in, w_out):
        for half in range(2):
            for t in range(half * FH, half * FH + FH):
                for o in (0, F):
                    out.append(blocks(w_in[:, o + t * P:o + t * P + P]))
            b = blocks(w_out[half * FH * P:(half + 1) * FH * P]).reshape(KT, P, FH, P)
            out.append(b.transpose(0, 2, 1, 3).reshape(FH, BLOCKS, P, P).transpose(0, 2, 1, 3).reshape(FH, P, SLAB))

    ffn(ffn_in[0], ffn_out[0])
    for m in range(KT):
        for o in (0, D, 2 * D):
            out.append(blocks(conv_in[:, o + m * P:o + m * P + P]))
    out.append(blocks(conv_out))
    ffn(ffn_in[1], ffn_out[1])
    stream = np.concatenate(out)
    assert stream.shape == (SLABS, P, SLAB)
    return stream


def kernel(x, c, attn_w_qkv, attn_w_o, conv_w_in, conv_w, conv_w_out, ada_w, ada_b, norm_mix_g, norm_ffn_g,
           ffn_w_in, ffn_w_out, final_g):
    import concourse.bacc as bacc
    from concourse.bass_utils import run_bass_kernel_spmd

    a = {k: np.asarray(v) for k, v in locals().items() if k not in ("bacc", "run_bass_kernel_spmd")}
    masks, rope, ident = constants()
    gains = np.concatenate([feature_major(g) for g in (a["norm_mix_g"][0], a["norm_ffn_g"][0], a["norm_mix_g"][1],
                                                       a["norm_ffn_g"][1], a["final_g"])], axis=1)
    arrays = {
        "xT": a["x"][0].T.reshape(KT, P, S).transpose(1, 0, 2),
        "cT": feature_major(a["c"][0]),
        "wstream": weight_stream(a["attn_w_qkv"][0], a["attn_w_o"][0], a["ffn_w_in"], a["ffn_w_out"],
                                 a["conv_w_in"][0], a["conv_w_out"][0]),
        "adaw": a["ada_w"].reshape(2, KT, P, 12, AJ).transpose(0, 3, 1, 2, 4).reshape(JOBS, KT, P, AJ),
        "adab": feature_major(a["ada_b"]),
        "gains": gains,
        "convw": a["conv_w"][0].reshape(3, KT, P).transpose(2, 1, 0).reshape(P, 3 * KT),
        "masks": masks,
        "rope": rope,
        "ident": ident,
    }
    arrays = {k: np.ascontiguousarray(v) for k, v in arrays.items()}
    nc = bacc.Bacc("TRN2", target_bir_lowering=False, num_devices=1)
    args = [nc.dram_tensor(k, v.shape, mybir.dt.from_np(v.dtype), kind="ExternalInput").ap() for k, v in arrays.items()]
    args.append(nc.dram_tensor("outT", (P, KT, S), F32, kind="ExternalOutput").ap())
    encoder(nc, *args)
    r = run_bass_kernel_spmd(nc, [arrays], core_ids=[0])
    return r.results[0]["outT"].transpose(1, 0, 2).reshape(D, S).T[None]
```
